# Optimizing a Trainium2 kernel written in Bass

```python
import math
import jax, jax.numpy as jnp
from jax import lax
import numpy as np

D_MODEL = 1024
BATCH = 1
SEQ = 1024
DEPTH = 1

CHUNK = 64
N_META = 16
W_CONV = 512
CONV_K = 3
N_Q_HEADS = 8
N_KV_HEADS = 2
HEAD_DIM = 64
Q_PER_KV = N_Q_HEADS // N_KV_HEADS
W_ATTN = N_Q_HEADS * HEAD_DIM
W_KV = N_KV_HEADS * HEAD_DIM
WINDOW = 128
WINDOW_CHUNKS = WINDOW // CHUNK
POOL_WINDOWS = (2, 4, 8, 16)
N_POOL_GROUPS = len(POOL_WINDOWS)
POOL_GROUP = 128
W_POOL = N_POOL_GROUPS * POOL_GROUP
N_BRANCH = 3
IN_SIZES = (W_CONV, W_CONV, W_CONV, W_CONV,
            W_ATTN, W_KV, W_KV, W_ATTN,
            W_POOL, W_POOL,
            N_BRANCH * D_MODEL)
W_IN = sum(IN_SIZES)
IN_SPLITS = tuple(int(s) for s in np.cumsum(IN_SIZES)[:-1])
ALPHA = (2 * DEPTH) ** 0.25
BETA = (8 * DEPTH) ** -0.25
LN_EPS = 1e-5
NEG_INF = -1e30

kernel_name = "hybrid_conv_swa_pool_deepnorm"

def _layer_norm(x, g, b):
    xf = x.astype(jnp.float32)
    mu = jnp.mean(xf, axis=-1, keepdims=True)
    var = jnp.mean(jnp.square(xf - mu), axis=-1, keepdims=True)
    y = (xf - mu) * lax.rsqrt(var + LN_EPS) * g.astype(jnp.float32) + b.astype(jnp.float32)
    return y.astype(x.dtype)

def _causal_depthwise_conv(u, w):
    L = u.shape[1]
    up = jnp.pad(u, ((0, 0), (CONV_K - 1, 0), (0, 0)))
    y = up[:, 0:L] * w[0]
    for j in range(1, CONV_K):
        y = y + up[:, j:j + L] * w[j]
    return y

def _sink_softmax(s, sink):
    m = jnp.maximum(jnp.max(s, axis=-1), sink)
    p = jnp.exp(s - m[..., None])
    denom = jnp.sum(p, axis=-1) + jnp.exp(sink - m)
    return p / denom[..., None]

def _sliding_sink_attention(q, k, v, sinks):
    Bn, L, _ = q.shape
    n_real = L - N_META
    n_chunks = n_real // CHUNK
    scale = 1.0 / math.sqrt(HEAD_DIM)
    sink = sinks.astype(jnp.float32).reshape(N_KV_HEADS, Q_PER_KV)

    q_meta = q[:, :N_META].reshape(Bn, N_META, N_KV_HEADS, Q_PER_KV, HEAD_DIM)
    k_meta = k[:, :N_META].reshape(Bn, N_META, N_KV_HEADS, HEAD_DIM)
    v_meta = v[:, :N_META].reshape(Bn, N_META, N_KV_HEADS, HEAD_DIM)
    q_real = q[:, N_META:].reshape(Bn, n_chunks, CHUNK, N_KV_HEADS, Q_PER_KV, HEAD_DIM)
    k_real = k[:, N_META:].reshape(Bn, n_chunks, CHUNK, N_KV_HEADS, HEAD_DIM)
    v_real = v[:, N_META:].reshape(Bn, n_chunks, CHUNK, N_KV_HEADS, HEAD_DIM)

    s_m = jnp.einsum('bqhgd,bkhd->bhgqk', q_meta, k_meta).astype(jnp.float32) * scale
    p_m = _sink_softmax(s_m, sink[None, :, :, None])
    o_meta = jnp.einsum('bhgqk,bkhd->bqhgd', p_m.astype(v.dtype), v_meta)
    o_meta = o_meta.reshape(Bn, N_META, W_ATTN)

    def shifted(t, j):
        return jnp.concatenate([jnp.zeros_like(t[:, :j]), t[:, :n_chunks - j]], axis=1)
    meta_k_b = jnp.broadcast_to(k_meta[:, None], (Bn, n_chunks, N_META, N_KV_HEADS, HEAD_DIM))
    meta_v_b = jnp.broadcast_to(v_meta[:, None], (Bn, n_chunks, N_META, N_KV_HEADS, HEAD_DIM))
    prev = list(range(WINDOW_CHUNKS - 1, 0, -1))
    keys = jnp.concatenate([meta_k_b] + [shifted(k_real, j) for j in prev] + [k_real], axis=2)
    vals = jnp.concatenate([meta_v_b] + [shifted(v_real, j) for j in prev] + [v_real], axis=2)
    c_idx = jnp.arange(n_chunks)[:, None]
    valid = [jnp.ones((n_chunks, N_META), bool)]
    valid += [jnp.broadcast_to(c_idx - j >= 0, (n_chunks, CHUNK)) for j in prev]
    valid += [jnp.ones((n_chunks, CHUNK), bool)]
    valid = jnp.concatenate(valid, axis=1)

    s_r = jnp.einsum('bcqhgd,bckhd->bchgqk', q_real, keys).astype(jnp.float32) * scale
    s_r = jnp.where(valid[None, :, None, None, None, :], s_r, NEG_INF)
    p_r = _sink_softmax(s_r, sink[None, None, :, :, None])
    o_real = jnp.einsum('bchgqk,bckhd->bcqhgd', p_r.astype(v.dtype), vals)
    o_real = o_real.reshape(Bn, n_real, W_ATTN)
    return jnp.concatenate([o_meta, o_real], axis=1)

def _multiscale_pool(u, pool_w, pool_scale):
    Bn, L, _ = u.shape
    ug = u.reshape(Bn, L, N_POOL_GROUPS, POOL_GROUP).astype(jnp.float32)
    cs0 = jnp.concatenate([jnp.zeros((Bn, 1, N_POOL_GROUPS, POOL_GROUP), jnp.float32),
                           jnp.cumsum(ug, axis=1)], axis=1)
    pos = jnp.arange(L)
    outs = []
    for g, w in enumerate(POOL_WINDOWS):
        c = cs0[:, :, g]
        lag = jnp.concatenate([jnp.zeros((Bn, w - 1, POOL_GROUP), jnp.float32), c[:, :L - w + 1]], axis=1)
        count = jnp.minimum(pos + 1, w).astype(jnp.float32)[None, :, None]
        outs.append((c[:, 1:] - lag) / count - ug[:, :, g])
    pooled = jnp.stack(outs, axis=2).astype(u.dtype)
    mapped = jnp.einsum('blgc,gcd->blgd', pooled, pool_w).reshape(Bn, L, W_POOL)
    return mapped * pool_scale

def _hybrid_layer(x, w_in, b_gate, conv_w, sinks, pool_w, pool_scale,
                  w_br_a, w_br_b, w_br_c, w_out, ln_g, ln_b):
    Bn, L, _ = x.shape
    proj = x @ w_in
    (a_b, a_c, a_h, a_z, q, k, v, b_z, c_u, c_z, g_logit) = jnp.split(proj, IN_SPLITS, axis=-1)
    y_a = a_b * _causal_depthwise_conv(a_c * a_h, conv_w) * jax.nn.silu(a_z)
    y_b = _sliding_sink_attention(q, k, v, sinks) * jax.nn.silu(b_z)
    y_c = _multiscale_pool(c_u, pool_w, pool_scale) * jax.nn.silu(c_z)
    gates = jax.nn.sigmoid(g_logit + b_gate).reshape(Bn, L, N_BRANCH, D_MODEL)
    merged = (gates[:, :, 0] * (y_a @ w_br_a)
              + gates[:, :, 1] * (y_b @ w_br_b)
              + gates[:, :, 2] * (y_c @ w_br_c))
    out = merged @ w_out
    return _layer_norm(ALPHA * x + out, ln_g, ln_b)

def setup_inputs(seed: int = 0) -> dict:
    key = jax.random.key(seed)
    ks = jax.random.split(key, 16)
    f32 = jnp.float32
    nrm = lambda k, shp, s: jax.random.normal(k, shp, f32) * s
    return {
        "x": nrm(ks[0], (BATCH, SEQ, D_MODEL), 1.0),
        "meta_tokens": nrm(ks[1], (N_META, D_MODEL), 1.0),
        "ln0_g": 1.0 + nrm(ks[2], (D_MODEL,), 0.02),
        "ln0_b": nrm(ks[3], (D_MODEL,), 0.02),
        "w_in": nrm(ks[4], (DEPTH, D_MODEL, W_IN), D_MODEL ** -0.5),
        "b_gate": nrm(ks[5], (DEPTH, N_BRANCH * D_MODEL), 0.02),
        "conv_w": nrm(ks[6], (DEPTH, CONV_K, W_CONV), CONV_K ** -0.5),
        "attn_sinks": nrm(ks[7], (DEPTH, N_Q_HEADS), 1.0),
        "pool_w": nrm(ks[8], (DEPTH, N_POOL_GROUPS, POOL_GROUP, POOL_GROUP), POOL_GROUP ** -0.5),
        "pool_scale": 1.0 + nrm(ks[9], (DEPTH, W_POOL), 0.02),
        "w_br_a": nrm(ks[10], (DEPTH, W_CONV, D_MODEL), BETA * W_CONV ** -0.5),
        "w_br_b": nrm(ks[11], (DEPTH, W_ATTN, D_MODEL), BETA * W_ATTN ** -0.5),
        "w_br_c": nrm(ks[12], (DEPTH, W_POOL, D_MODEL), BETA * W_POOL ** -0.5),
        "w_out": nrm(ks[13], (DEPTH, D_MODEL, D_MODEL), BETA * D_MODEL ** -0.5),
        "ln_g": 1.0 + nrm(ks[14], (DEPTH, D_MODEL), 0.02),
        "ln_b": nrm(ks[15], (DEPTH, D_MODEL), 0.02),
    }

def reference(x, meta_tokens, ln0_g, ln0_b, w_in, b_gate, conv_w, attn_sinks, pool_w,
              pool_scale, w_br_a, w_br_b, w_br_c, w_out, ln_g, ln_b):
    Bn = x.shape[0]
    meta = jnp.broadcast_to(meta_tokens[None].astype(x.dtype), (Bn, N_META, D_MODEL))
    h = _layer_norm(jnp.concatenate([meta, x], axis=1), ln0_g, ln0_b)
    for i in range(DEPTH):
        h = _hybrid_layer(h, w_in[i], b_gate[i], conv_w[i], attn_sinks[i], pool_w[i],
                          pool_scale[i], w_br_a[i], w_br_b[i], w_br_c[i], w_out[i],
                          ln_g[i], ln_b[i])
    return h[:, N_META:]


_drawn_inputs = setup_inputs


def setup_inputs(seed=0):
    import zlib

    import numpy as np

    out = dict(_drawn_inputs(seed))
    spreads = {}
    factors = {'meta_tokens': 8.0,
     'ln0_g': 2.741,
     'ln0_b': 2.949,
     'b_gate': 8.0,
     'attn_sinks': 64.0,
     'pool_scale': 36.761,
     'w_br_b': 4.212,
     'ln_g': 8.265,
     'ln_b': 8.243}
    for name, (base, spread) in spreads.items():
        noise = np.random.default_rng([zlib.crc32(name.encode()), seed]).standard_normal(out[name].shape)
        drawn = base * np.exp(spread * noise) if base else spread * noise
        out[name] = __import__('jax').numpy.asarray(drawn.astype(out[name].dtype))
    for name, factor in factors.items():
        out[name] = (out[name] * factor).astype(out[name].dtype)
    return out
```

```python
from contextlib import ExitStack

import concourse.bass as bass
from concourse import mybir

F32 = mybir.dt.float32
F32R = mybir.dt.float32r
ALU = mybir.AluOpType
ACT = mybir.ActivationFunctionType
AX_X = mybir.AxisListType.X

P = 128
D = 1024
KC = D // P
SEQ = 1024
META = 16
TOK = META + SEQ
CHUNK = 64
N_CHUNKS = SEQ // CHUNK
HEAD = 64
PAD = CHUNK
KEYS = META + 2 * CHUNK
LN_EPS = 1e-5
NEG_INF = -1e30
ALPHA = 2 ** 0.25
SCALE = HEAD ** -0.5
POOL_WINDOWS = (2, 4, 8, 16)
N_BRANCH = 3
HALF = 512

COL_AB, COL_AC, COL_AH, COL_AZ = 0, 512, 1024, 1536
COL_Q, COL_K, COL_V, COL_BZ = 2048, 2560, 2688, 2816
COL_CU, COL_CZ, COL_GATE = 3328, 3840, 4352

WITH_META = ((0, 348), (348, 694), (694, TOK))
REAL_ONLY = ((META, META + HALF), (META + HALF, TOK))

SCORES_AFTER = (-1, 2, 5, 7)
TURN_AFTER = (1, 4, 7, 9)
TIMES_V_AFTER = (2, 5, 8, 10)
N_ZEROED = 6

ROW_G0, ROW_B0, ROW_BG, ROW_CONV, ROW_PS = 0, 8, 16, 40, 52
N_ROWS = 56


class Section:

    def __init__(self, before, banks, tiles, turns):
        self.tile0 = before.tile_end if before else 0
        self.group0 = before.group_end if before else 0
        self.used0 = list(before.used_end) if before else [0] * 4
        self.banks, self.tiles, self.turns = banks, tiles, turns
        self.per_turn = [banks.count(b) for b in range(4)]
        self.tile_end = self.tile0 + tiles * turns
        self.group_end = self.group0 + len(banks) * turns
        self.used_end = [u + n * turns for u, n in zip(self.used0, self.per_turn)]

    def tile(self, turn, n):
        return turn * self.tiles + (self.tile0 + n)

    def groups(self, turn, g):
        return turn * len(self.banks) + (self.group0 + g)

    def used(self, turn, g):
        b = self.banks[g]
        return turn * self.per_turn[b] + (self.used0[b] + self.banks[:g].count(b))


def wait(eng, sem, value):
    if not isinstance(value, int) or value > 0:
        eng.wait_ge(sem, value)


def hybrid_layer(nc, x, meta_tokens, ln0_g, ln0_b, w_in, b_gate, conv_w, attn_sinks, pool_w, pool_scale,
                 w_br_a, w_br_b, w_br_c, w_out, ln_g, ln_b, out):
    KV = Section(None, (0, 1, 2, 0, 1, 2), 2, 1)
    Q = Section(KV, (0, 1, 2, 1), 2, 2)
    MIX = Section(Q, (0, 1, 2, 0, 1, 2, 0, 1, 2, 0, 1), 4, 4)
    MAP = Section(MIX, (0, 1, 2, 3, 0, 1, 2, 3), 0, 1)
    Z, GATE = [], []
    last = MAP
    for _ in range(N_BRANCH):
        Z.append(Section(last, (0, 1, 2, 3), 2, 2))
        GATE.append(Section(Z[-1], (0, 1, 2, 3) * 4, 6, 2))
        last = GATE[-1]
    N_TILES = last.tile_end
    GROUPS_IN = last.group_end
    BRANCH_TILES = GATE[0].tile_end - Z[0].tile0
    BRANCH_GROUPS = GATE[0].group_end - Z[0].group0
    BRANCH_USES = GATE[0].used_end[0] - Z[0].used0[0]
    OUT_PIECES = 8
    OUT_SPLITS = [("m", 0), ("w", 0), ("m", 1), ("w", 1), ("m", 2), ("m", 3), ("w", 2), ("w", 3),
                  ("m", 4), ("m", 5), ("m", 6), ("m", 7), ("w", 4), ("w", 5), ("w", 6), ("w", 7)]
    T_TILES = SEQ // P

    with ExitStack() as ctx:
        def sb(name, shape, dt=F32, stack=ctx):
            return stack.enter_context(nc.sbuf_tensor(name, shape, dt))

        def sem(name):
            return ctx.enter_context(nc.semaphore(name))

        h_hi = sb("h_hi", [P, KC, TOK], F32R)
        h_lo = sb("h_lo", [P, KC, TOK], F32R)
        raw = sb("raw", [P, 2, KC, P])
        w_hi = sb("w_hi", [P, 2, KC, P], F32R)
        w_lo = sb("w_lo", [P, 2, KC, P], F32R)
        merged = sb("merged", [P, KC, SEQ])
        ident = sb("ident", [P, P])
        params = sb("params", [P, N_ROWS])
        rstd = sb("rstd", [P, 1 + T_TILES])
        nmr = sb("nmr", [P, 1 + T_TILES])
        gate_bias = sb("gate_bias", [P, 4])

        conv_out = merged[:, 0:4, :]
        xin = merged

        def column(row):
            return params[:, row:row + 1]

        qm = ExitStack()
        q_o = sb("q_o", [P, 4, SEQ], stack=qm)
        pooled = sb("pooled", [P, 4, SEQ], stack=qm)
        hf = q_o[:, :, 0:HALF]
        xmeta = pooled[0:META, 0, :]
        prow = pooled[0:N_ROWS, 1, 0:P]
        hfm = pooled[:, 2, 0:P].rearrange("p (k m) -> p k m", m=META)

        one = ExitStack()
        kT = sb("kT", [P, META + PAD + SEQ], stack=one)
        vT = sb("vT", [P, META + PAD + SEQ], stack=one)
        v_win = sb("v_win", [P, N_CHUNKS, P], stack=one)
        v_meta_bd = sb("v_meta_bd", [2 * META, P], stack=one)
        vT_meta_bd = sb("vT_meta_bd", [P, 2 * META], stack=one)
        q_stage = sb("q_stage", [P, 4, CHUNK], stack=one)
        k_stage = sb("k_stage", [P, 2 * KEYS], stack=one)
        v_stage = sb("v_stage", [P, 3, HEAD], stack=one)
        probs = sb("probs", [P, 2, 2 * KEYS], stack=one)
        pT = sb("pT", [P, 2, 2, P], stack=one)
        pT_meta = sb("pT_meta", [2 * META, 2, P], stack=one)
        ac_sb = sb("ac_sb", [P, TOK], stack=one)
        u_sb = sb("u_sb", [P, TOK], stack=one)
        cu_sb = sb("cu_sb", [P, TOK], stack=one)
        win_a = sb("win_a", [P, TOK], stack=one)
        win_b = sb("win_b", [P, TOK], stack=one)
        pool_wt = sb("pool_wt", [P, 4, P], stack=one)
        small = sb("small", [P, 8, 16], stack=one)
        stats = sb("stats", [P, 1 + T_TILES, 2, 6], stack=one)
        mv = sb("mv", [P, 1 + T_TILES, 2], stack=one)
        neg_sink = sb("neg_sink", [P, 4], stack=one)
        sink = sb("sink", [P, 4], stack=one)
        all_sinks = sb("all_sinks", [P, 8], stack=one)
        one.close()
        row_max, neg_m, sink_m, sink_e = (small[:, n, 0:4] for n in range(4))
        row_sum, denom, r_den = (small[:, n, 0:4] for n in range(4, 7))

        two = ExitStack()
        y_hi = sb("y_hi", [P, 4, SEQ], F32R, stack=two)
        y_lo = sb("y_lo", [P, 4, SEQ], F32R, stack=two)
        silu = sb("silu", [P, 2, HALF], stack=two)
        y_f = sb("y_f", [P, 2, HALF], stack=two)
        sig = sb("sig", [P, 2, SEQ], stack=two)
        two.close()
        qm.close()

        three = ExitStack()
        wo_hi0 = sb("wo_hi0", [P, KC, HALF], F32R, stack=three)
        wo_lo0 = sb("wo_lo0", [P, KC, HALF], F32R, stack=three)
        wo_hi1 = sb("wo_hi1", [P, KC, HALF], F32R, stack=three)
        wo_lo1 = sb("wo_lo1", [P, KC, HALF], F32R, stack=three)
        hz = sb("hz", [P, 2, D], stack=three)
        stats2 = sb("stats2", [P, T_TILES, 2, 6], stack=three)
        mv2 = sb("mv2", [P, T_TILES, 2], stack=three)
        small2 = sb("small2", [P, 8, T_TILES], stack=three)
        three.close()
        wo_hi, wo_lo = (wo_hi0, wo_hi1), (wo_lo0, wo_lo1)
        gain0, bias0, gain1, bias1 = (merged[:, n, :] for n in range(4))
        xr = merged[:, 4:6, :]
        res = merged[:, 6:8, :]

        PS = ctx.enter_context(nc.psum_tensor("PS", [P, 8, HALF], F32))
        S_PS = PS[:, 3:5, 0:2 * KEYS]
        PT_PS = PS[:, 5, :].rearrange("p (g c r) -> p g c r", g=2, c=2)
        PTM_PS = PS[0:2 * META, 6, 0:2 * P].rearrange("p (c r) -> p c r", c=2)
        O_PS = PS[:, 7, 0:4 * CHUNK].rearrange("p (t q) -> p t q", t=4)
        META_COLS = slice(2 * CHUNK, 2 * CHUNK + 2 * META)
        WIN_COLS = (slice(0, 2 * CHUNK), slice(KEYS + META, 2 * KEYS))

        x_loaded = [sem(f"x_loaded{n}") for n in range(1 + T_TILES)]
        params_loaded = sem("params_loaded")
        sinks_loaded = sem("sinks_loaded")
        pool_w_loaded = sem("pool_w_loaded")
        raw_loaded = [sem(f"raw_loaded{s}") for s in range(2)]
        ident_ready = sem("ident_ready")
        zeroed = sem("zeroed")
        params_turned = sem("params_turned")
        params_ready = sem("params_ready")
        dve_step = sem("dve_step")
        var_ready = sem("var_ready")
        root_ready = sem("root_ready")
        rstd_ready = sem("rstd_ready")
        z_ready = sem("z_ready")
        z_turned = sem("z_turned")
        hf_ready = sem("hf_ready")
        h_hi_ready = sem("h_hi_ready")
        h_lo_ready = sem("h_lo_ready")
        w_hi_ready = sem("w_hi_ready")
        w_lo_ready = sem("w_lo_ready")
        groups_done = sem("groups_done")
        bank_read = [sem(f"bank_read{b}") for b in range(4)]
        v_turned = sem("v_turned")
        v_win_ready = sem("v_win_ready")
        v_meta_ready = sem("v_meta_ready")
        meta_staged = sem("meta_staged")
        qk_staged = sem("qk_staged")
        v_staged = sem("v_staged")
        scores_done = sem("scores_done")
        neg_m_ready = sem("neg_m_ready")
        sink_m_ready = sem("sink_m_ready")
        probs_ready = sem("probs_ready")
        sink_e_ready = sem("sink_e_ready")
        probs_scaled = sem("probs_scaled")
        probs_turned = sem("probs_turned")
        pT_ready = sem("pT_ready")
        pT_meta_ready = sem("pT_meta_ready")
        o_done = sem("o_done")
        o_ready = sem("o_ready")
        conv_ready = sem("conv_ready")
        conv_step = sem("conv_step")
        pool_step = sem("pool_step")
        pooled_ready = sem("pooled_ready")
        y_f_ready = sem("y_f_ready")
        gate_bias_ready = sem("gate_bias_ready")
        y_hi_ready = sem("y_hi_ready")
        y_lo_ready = sem("y_lo_ready")
        merged_step = sem("merged_step")
        m_hi_ready = sem("m_hi_ready")
        m_lo_ready = sem("m_lo_ready")
        wo_hi_ready = sem("wo_hi_ready")
        wo_lo_ready = sem("wo_lo_ready")
        rows_loaded = sem("rows_loaded")
        gain_scaled = sem("gain_scaled")
        xr_loaded = [sem(f"xr_loaded{s}") for s in range(2)]
        hz_ready = sem("hz_ready")
        skip_step = sem("skip_step")
        skip_ready = sem("skip_ready")
        out_done = sem("out_done")
        res_half = sem("res_half")
        var2_ready = sem("var2_ready")
        root2_ready = sem("root2_ready")
        rstd2_ready = sem("rstd2_ready")
        norm_ready = sem("norm_ready")
        tail_step = sem("tail_step")
        row_ready = sem("row_ready")
        stored = [sem(f"stored{s}") for s in range(2)]

        def two_turns(eng, body, apart):
            if apart:
                body(0)
                body(1)
            else:
                with eng.Fori(0, 2) as i:
                    body(i)

        block = ctx.enter_context(nc.Block())

        w_view = w_in[0].rearrange("(k p) n -> p k n", p=P)

        def token_col(t):
            return t if t < META else t + PAD

        def kv_parts(a, b):
            if a < META:
                return ((0, META - a, token_col(a)), (META - a, b - a, token_col(META)))
            return ((0, b - a, token_col(a)),)

        @block.sync
        def _(sp):
            x_rows = x[0].rearrange("(t p) d -> t p d", p=P)
            sp.dma_start(xmeta, meta_tokens).then_inc(x_loaded[0], 16)
            for t in range(4):
                sp.dma_start(xin[:, t, :], x_rows[t]).then_inc(x_loaded[1 + t], 16)
            for row, src in ((ROW_G0, ln0_g.rearrange("(r c) -> r c", c=P)),
                             (ROW_B0, ln0_b.rearrange("(r c) -> r c", c=P)),
                             (ROW_BG, b_gate[0].rearrange("(r c) -> r c", c=P)),
                             (ROW_CONV, conv_w[0].rearrange("j (r c) -> (j r) c", c=P)),
                             (ROW_PS, pool_scale[0].rearrange("(r c) -> r c", c=P))):
                sp.dma_start(prow[row:row + src.shape[0], :], src).then_inc(params_loaded, 16)
            for t in range(4, T_TILES):
                sp.dma_start(xin[:, t, :], x_rows[t]).then_inc(x_loaded[1 + t], 16)

            def load_columns(tile, slot, col):
                raw_free(tile)
                for k in (4, 0):
                    sp.dma_start(raw[:, slot, k:k + 4, :], w_view[:, k:k + 4, bass.ds(col, P)])\
                        .then_inc(raw_loaded[slot], 16)

            def load_heads(tile, slot, col):
                raw_free(tile)
                for half in range(2):
                    sp.dma_start(raw[:, slot, :, HEAD * half:HEAD * (half + 1)],
                                 w_view[:, :, bass.ds(col + 256 * half, HEAD)])\
                        .then_inc(raw_loaded[slot], 16)

            def raw_free(tile):
                if isinstance(tile, int) and tile < 2:
                    return
                sp.wait_ge(w_hi_ready, tile - 1)
                sp.wait_ge(w_lo_ready, tile - 1)

            load_columns(0, 0, COL_K)
            load_columns(1, 1, COL_V)
            sp.dma_start(all_sinks[:], attn_sinks[0:1, :].partition_broadcast(P)).then_inc(sinks_loaded, 16)
            sp.dma_start(pool_wt[:], pool_w[0].rearrange("g c d -> c g d")).then_inc(pool_w_loaded, 16)
            with sp.Fori(0, 2) as i:
                for n in range(2):
                    load_heads(Q.tile(i, n), n, i * (2 * HEAD) + (COL_Q + HEAD * n))
            with sp.Fori(0, 4) as i:
                for n, col in enumerate((COL_CU, COL_AC, COL_AH, COL_AB)):
                    load_columns(MIX.tile(i, n), n % 2, i * P + col)
            for b, (col_z, w_br) in enumerate(((COL_AZ, w_br_a), (COL_BZ, w_br_b), (COL_CZ, w_br_c))):
                with sp.Fori(0, 2) as i:
                    for n in range(2):
                        if b == 1:
                            load_heads(Z[b].tile(i, n), n, i * (2 * HEAD) + (col_z + HEAD * n))
                        else:
                            load_columns(Z[b].tile(i, n), n, i * (2 * P) + (col_z + P * n))
                with sp.Fori(0, 2) as i:
                    for pair in range(2):
                        for n in range(2):
                            tile = GATE[b].tile(i, 3 * pair + n)
                            load_columns(tile, (3 * pair + n) % 2,
                                         i * (4 * P) + (COL_GATE + D * b + P * (2 * pair + n)))
                        n = 3 * pair + 2
                        raw_free(GATE[b].tile(i, n))
                        dst = raw[:, n % 2, :, :].rearrange("p (k two) c -> p k (two c)", two=2)
                        for half in (1, 0):
                            rows = (w_br[0, 256 * half:256 * half + 256, :].rearrange("(k p) n -> p k n", p=64)
                                    if b == 1 else
                                    w_br[0].rearrange("(k p) n -> p k n", p=P)[64 * half:64 * half + 64])
                            sp.dma_start(dst[64 * half:64 * half + 64],
                                         rows[:, :, bass.ds(i * (4 * P) + 2 * P * pair, 2 * P)])\
                                .then_inc(raw_loaded[n % 2], 16)
            wo_view = w_out[0].rearrange("(k p) n -> p k n", p=P)
            for n in range(OUT_PIECES):
                half, k = n // 4, 2 * (n % 4)
                if n < 2:
                    raw_free(N_TILES + n)
                else:
                    sp.wait_ge(wo_hi_ready, n - 1)
                    sp.wait_ge(wo_lo_ready, n - 1)
                dst = raw[:, n % 2, :, :].rearrange("p (k four) c -> p k (four c)", four=4)
                for j in range(2):
                    sp.dma_start(dst[:, j, :], wo_view[:, k + j, HALF * half:HALF * half + HALF])\
                        .then_inc(raw_loaded[n % 2], 16)
            sp.wait_ge(m_hi_ready, T_TILES)
            sp.wait_ge(m_lo_ready, T_TILES)
            for dst, src in ((gain0, ln0_g), (bias0, ln0_b), (gain1, ln_g[0]), (bias1, ln_b[0])):
                sp.dma_start(dst, src.rearrange("(a n) -> a n", a=1).partition_broadcast(P))\
                    .then_inc(rows_loaded, 16)
            out_rows = out[0].rearrange("(t p) d -> t p d", p=P)
            for t in range(2):
                sp.dma_start(xr[:, t, :], x_rows[t]).then_inc(xr_loaded[t], 16)
            for t in range(T_TILES):
                if t + 2 < T_TILES:
                    sp.wait_ge(hz_ready, t + 1)
                    sp.dma_start(xr[:, t % 2, :], x_rows[t + 2]).then_inc(xr_loaded[t % 2], 16)
                sp.wait_ge(row_ready, t + 1)
                sp.dma_start(out_rows[t], res[:, t % 2, :]).then_inc(stored[t % 2], 16)
            for s in range(2):
                sp.wait_ge(stored[s], 16 * (T_TILES // 2))

        @block.gpsimd
        def _(pool):
            g = nc.gpsimd
            g.memset(ident[:], 0.0).then_inc(ident_ready, 1)
            g.memset(mv[:], 1.0).then_inc(zeroed, 1)
            pool.wait_ge(ident_ready, 1)
            g.affine_select(out=ident[:], in_=ident[:], compare_op=ALU.not_equal, fill=1.0, base=0,
                            pattern=[[-1, P]], channel_multiplier=1).then_inc(ident_ready, 1)
            g.memset(kT[:, META:META + PAD], 0.0).then_inc(zeroed, 1)
            g.memset(vT[:, META:META + PAD], 0.0).then_inc(zeroed, 1)
            g.memset(k_stage[:], 0.0).then_inc(zeroed, 1)
            g.memset(v_stage[:], 0.0).then_inc(zeroed, 1)
            g.memset(vT_meta_bd[:], 0.0).then_inc(zeroed, 1)
            for n in range(2 * KC):
                half, k = n // KC, n % KC
                pool.wait_ge(h_hi_ready, n + 1)
                cols = slice(META + HALF * half, META + HALF * half + HALF)
                g.tensor_tensor(h_lo[:, k, cols], hf[:, n % 4, :], h_hi[:, k, cols].bitcast(F32),
                                ALU.subtract).then_inc(h_lo_ready, 1)
            pool.wait_ge(h_hi_ready, 2 * KC + 1)
            g.tensor_tensor(h_lo[:, :, 0:META], hfm, h_hi[:, :, 0:META].bitcast(F32), ALU.subtract)\
                .then_inc(h_lo_ready, 1)

            step = 0
            for i, w in enumerate(POOL_WINDOWS):
                for n in range(3):
                    pool.wait_ge(bank_read[MIX.banks[n]], MIX.used(i, n) + 1)
                src, size = cu_sb, 1
                for dst in (win_a, win_b, win_a, win_b)[:i + 1]:
                    lead = 2 * size - 1
                    g.tensor_tensor(dst[:, lead:TOK], src[:, lead:TOK], src[:, lead - size:TOK - size],
                                    ALU.add).then_inc(pool_step, 1)
                    step += 1
                    pool.wait_ge(pool_step, step)
                    src, size = dst, 2 * size
                g.tensor_scalar(src[:, META:TOK], src[:, META:TOK], 1.0 / w, None, ALU.mult)\
                    .then_inc(pool_step, 1)
                step += 1
                pool.wait_ge(pool_step, step)
                g.tensor_tensor(pooled[:, i, :], src[:, META:TOK], cu_sb[:, META:TOK], ALU.subtract)\
                    .then_inc(pooled_ready, 1)

            pool.wait_ge(rows_loaded, 64)
            g.tensor_scalar(gain0, gain0, ALPHA, None, ALU.mult).then_inc(gain_scaled, 1)
            g.tensor_scalar(bias0, bias0, ALPHA, None, ALU.mult).then_inc(gain_scaled, 1)
            pool.wait_ge(gain_scaled, 2)
            for t in range(T_TILES):
                pool.wait_ge(hz_ready, t + 1)
                g.tensor_tensor(hz[:, t % 2, :], hz[:, t % 2, :], gain0, ALU.mult).then_inc(skip_step, 1)
                pool.wait_ge(skip_step, t + 1)
                g.tensor_tensor(hz[:, t % 2, :], hz[:, t % 2, :], bias0, ALU.add).then_inc(skip_ready, 1)

        def split_hi(act, tile, slot, groups_before):
            n = tile // 2 if isinstance(tile, int) else None
            act.wait_ge(raw_loaded[slot], raw_count(tile, slot))
            if groups_before is not None:
                act.wait_ge(groups_done, groups_before)
            nc.scalar.activation(w_hi[:, slot], raw[:, slot], ACT.Copy).then_inc(w_hi_ready, 1)

        def split_lo(dve, tile, slot, groups_before):
            dve.wait_ge(raw_loaded[slot], raw_count(tile, slot))
            dve.wait_ge(w_hi_ready, tile + 1)
            if groups_before is not None:
                dve.wait_ge(groups_done, groups_before)
            nc.vector.tensor_tensor(w_lo[:, slot], raw[:, slot], w_hi[:, slot].bitcast(F32),
                                    ALU.subtract).then_inc(w_lo_ready, 1)

        def raw_count(tile, slot):
            return tile * 16 + (32 - 16 * slot)

        def split_next(eng, split, sec, turn, n, g):
            split(eng, sec.tile(turn, n) + 1, (n + 1) % 2, sec.groups(turn, g))

        def out_part(parts, n):
            half, k = n // 4, 2 * (n % 4)
            return (parts[half][:, k:k + 2, :],
                    raw[:, n % 2, :, :].rearrange("p (k four) c -> p k (four c)", four=4))

        def split_out_hi(act, n):
            act.wait_ge(raw_loaded[n % 2], raw_count(N_TILES + n, n % 2))
            dst, src = out_part(wo_hi, n)
            nc.scalar.activation(dst, src, ACT.Copy).then_inc(wo_hi_ready, 1)

        def split_out_lo(dve, n):
            dve.wait_ge(raw_loaded[n % 2], raw_count(N_TILES + n, n % 2))
            dve.wait_ge(wo_hi_ready, n + 1)
            dst, src = out_part(wo_lo, n)
            hi, _ = out_part(wo_hi, n)
            nc.vector.tensor_tensor(dst, src, hi.bitcast(F32), ALU.subtract).then_inc(wo_lo_ready, 1)

        def out_count(t, h):
            return 4 * h + t + 1 if t < 4 else 8 + 2 * (t - 4) + h + 1

        @block.scalar
        def _(act):
            s = nc.scalar

            def root(n):
                act.wait_ge(var_ready, n + 1)
                cols = slice(0, 5) if n == 0 else slice(5, 9)
                s.activation(small[:, 0, cols], mv[:, cols, 1], ACT.Sqrt).then_inc(root_ready, 1)

            def normalise(c):
                part = xmeta if c == 0 else xin[:, c - 1, :]
                rows = META if c == 0 else P
                s.activation(part, part, ACT.Identity, bias=nmr[0:rows, c:c + 1], scale=rstd[0:rows, c:c + 1])\
                    .then_inc(z_ready, 1)

            def h_hi_block(n):
                half, k = n // KC, n % KC
                act.wait_ge(hf_ready, n + 1)
                s.activation(h_hi[:, k, META + HALF * half:META + HALF * half + HALF], hf[:, n % 4, :],
                             ACT.Copy).then_inc(h_hi_ready, 1)

            root(0)
            act.wait_ge(rstd_ready, 1)
            for c in (1, 2, 3, 4, 0):
                normalise(c)
            root(1)
            act.wait_ge(rstd_ready, 2)
            for c in range(5, 9):
                normalise(c)
            for n in range(KC):
                h_hi_block(n)
            split_hi(act, 0, 0, None)
            for n in range(KC, 2 * KC):
                h_hi_block(n)
            act.wait_ge(hf_ready, 2 * KC + 1)
            s.activation(h_hi[:, :, 0:META], hfm, ACT.Copy).then_inc(h_hi_ready, 1)

            def read_group(sec, turn, g, dst, func=ACT.Copy, src_cols=None, last=True, **kw):
                b = sec.banks[g]
                a, z = src_cols
                ins = s.activation(dst, PS[:, b, a:z], func, **kw)
                if last:
                    ins.then_inc(bank_read[b], 1)

            for n, dst in enumerate((kT, vT)):
                if n == 0:
                    split_hi(act, 1, 1, None)
                else:
                    split_next(act, split_hi, KV, 0, 1, 3)
                for c, (a, b) in enumerate(WITH_META):
                    g = 3 * n + c
                    act.wait_ge(groups_done, KV.groups(0, g) + 1)
                    parts = kv_parts(a, b)
                    for m, (p0, p1, col) in enumerate(parts):
                        read_group(KV, 0, g, dst[:, col:col + p1 - p0], src_cols=(p0, p1),
                                   last=m == len(parts) - 1)
            act.wait_ge(zeroed, N_ZEROED)
            for b in range(3):
                act.wait_ge(bank_read[b], KV.used_end[b])
            for g in range(2):
                rows, cols = slice(64 * g, 64 * g + 64), slice(META * g, META * g + META)
                s.activation(vT_meta_bd[rows, cols], vT[rows, 0:META], ACT.Copy).then_inc(meta_staged, 1)
                s.activation(k_stage[rows, META_COLS][:, cols], kT[rows, 0:META], ACT.Copy)\
                    .then_inc(meta_staged, 1)
            with act.Fori(0, 2) as i:
                for n in range(2):
                    split_next(act, split_hi, Q, i, n, 2 * n)
                    for c in range(2):
                        g = 2 * n + c
                        act.wait_ge(groups_done, Q.groups(i, g) + 1)
                        read_group(Q, i, g, q_o[:, bass.ds(i * 2 + n, 1), HALF * c:HALF * c + HALF],
                                   src_cols=(0, HALF))

            def stage_qk(i, n):
                chunk = i * 4 + n
                wait(act, scores_done, chunk)
                s.activation(q_stage[:], q_o[:, :, bass.ds(chunk * CHUNK, CHUNK)], ACT.Copy)\
                    .then_inc(qk_staged, 1)
                for g in range(2):
                    rows = slice(64 * g, 64 * g + 64)
                    s.activation(k_stage[rows, WIN_COLS[g]], kT[rows, bass.ds(chunk * CHUNK + META, 2 * CHUNK)],
                                 ACT.Copy).then_inc(qk_staged, 1)

            def stage_v(i, n):
                chunk = i * 4 + n
                wait(act, o_done, chunk)
                s.activation(v_stage[:, 0:3:2, :],
                             v_win[:, bass.ds(chunk, 1), :].rearrange("p w (g d) -> p (w g) d", g=2),
                             ACT.Copy).then_inc(v_staged, 1)

            def softmax_exp(i, n):
                chunk = i * 4 + n
                act.wait_ge(neg_m_ready, chunk + 1)
                wait(act, probs_turned, chunk)
                for c in range(2):
                    for g in range(2):
                        j, cols = 2 * c + g, slice(KEYS * g, KEYS * g + KEYS)
                        s.activation(probs[:, c, cols], S_PS[:, c, cols], ACT.Exp,
                                     bias=neg_m[:, j:j + 1], scale=SCALE, accum_out=row_sum[:, j:j + 1])\
                            .then_inc(probs_ready, 1)
                act.wait_ge(sink_m_ready, chunk + 1)
                s.activation(sink_e, sink_m, ACT.Exp).then_inc(sink_e_ready, 1)

            def copy_pT_meta(i, n):
                chunk = i * 4 + n
                act.wait_ge(probs_turned, chunk + 1)
                wait(act, o_done, chunk)
                s.activation(pT_meta[:], PTM_PS, ACT.Copy).then_inc(pT_meta_ready, 1)

            for b in range(3):
                act.wait_ge(bank_read[b], Q.used_end[b])
            act.wait_ge(v_win_ready, 4)

            def mix_turn(i):
                stage_qk(i, 0)
                softmax_exp(i, 0)
                stage_qk(i, 1)
                for g in range(11):
                    tile, c = min(g // 3, 3), g - 3 * min(g // 3, 3)
                    if c == 0:
                        split_next(act, split_hi, MIX, i, tile, g)
                    if tile < 2:
                        a, b = WITH_META[c]
                        act.wait_ge(groups_done, MIX.groups(i, g) + 1)
                        if tile == 0:
                            wait(act, pooled_ready, i)
                        else:
                            wait(act, conv_ready, i)
                        read_group(MIX, i, g, (cu_sb, ac_sb)[tile][:, a:b], src_cols=(0, b - a))
                    if g in TURN_AFTER:
                        stage_v(i, TURN_AFTER.index(g))
                        copy_pT_meta(i, TURN_AFTER.index(g))
                    if g in SCORES_AFTER:
                        n = SCORES_AFTER.index(g)
                        softmax_exp(i, n)
                        if n < 3:
                            stage_qk(i, n + 1)

            mix_turn(0)
            with act.Fori(1, 4) as i:
                mix_turn(i)

            for b in range(N_BRANCH):
                def z_turn(i):
                    for n in range(2):
                        split_next(act, split_hi, Z[b], i, n, 2 * n)
                        k = i * 2 + n
                        for c in range(2):
                            g = 2 * n + c
                            act.wait_ge(groups_done, Z[b].groups(i, g) + 1)
                            wait(act, y_f_ready, k * 2 + (8 * b + c - 1))
                            read_group(Z[b], i, g, silu[:, c, :], ACT.Silu, src_cols=(0, HALF))
                        for c in range(2):
                            act.wait_ge(y_f_ready, k * 2 + (8 * b + c + 1))
                            s.activation(y_hi[:, bass.ds(k, 1), HALF * c:HALF * c + HALF],
                                         y_f[:, bass.ds(c, 1), :], ACT.Copy).then_inc(y_hi_ready, 1)
                two_turns(act, z_turn, apart=b == 0)

                def gate_turn(i):
                    wait(act, merged_step, i * 8 + 16 * b)
                    s.activation(gate_bias[:], params[:, bass.ds(i * 4 + (ROW_BG + 8 * b), 4)], ACT.Copy)\
                        .then_inc(gate_bias_ready, 1)
                    act.wait_ge(gate_bias_ready, i + (2 * b + 1))
                    for pair in range(2):
                        for n in range(2):
                            tile, g = 3 * pair + n, 8 * pair + 2 * n
                            split_next(act, split_hi, GATE[b], i, tile, g)
                            for c in range(2):
                                act.wait_ge(groups_done, GATE[b].groups(i, g + c) + 1)
                                wait(act, merged_step, i * 8 + (16 * b + 4 * pair))
                                s.activation(sig[:, n, HALF * c:HALF * c + HALF], PS[:, GATE[b].banks[g + c], :],
                                             ACT.Sigmoid,
                                             bias=gate_bias[:, 2 * pair + n:2 * pair + n + 1])\
                                    .then_inc(bank_read[GATE[b].banks[g + c]], 1)
                        if not (b == N_BRANCH - 1 and isinstance(i, int) and i == 1 and pair == 1):
                            split_next(act, split_hi, GATE[b], i, 3 * pair + 2, 8 * pair + 4)

                two_turns(act, gate_turn, apart=b != 1)

            act.wait_ge(merged_step, 16 * N_BRANCH)
            act.wait_ge(groups_done, GROUPS_IN)
            for kind, n in OUT_SPLITS:
                if kind == "w":
                    split_out_hi(act, n)
                else:
                    s.activation(h_hi[:, :, META + P * n:META + P * n + P], merged[:, :, P * n:P * n + P],
                                 ACT.Copy).then_inc(m_hi_ready, 1)

            def skip_rows(t):
                act.wait_ge(xr_loaded[t % 2], 16 * (t // 2 + 1))
                if t >= 2:
                    act.wait_ge(res_half, 2 * t - 2)
                s.activation(hz[:, t % 2, :], xr[:, t % 2, :], ACT.Identity,
                             bias=nmr[:, t + 1:t + 2], scale=rstd[:, t + 1:t + 2]).then_inc(hz_ready, 1)

            skip_rows(0)
            skip_rows(1)
            for t in range(T_TILES):
                act.wait_ge(var2_ready, t + 1)
                s.activation(small2[:, 1, t:t + 1], small2[:, 0, t:t + 1], ACT.Sqrt).then_inc(root2_ready, 1)
                act.wait_ge(rstd2_ready, t + 1)
                s.activation(res[:, t % 2, :], res[:, t % 2, :], ACT.Identity,
                             bias=small2[:, 4, t:t + 1], scale=small2[:, 2, t:t + 1]).then_inc(norm_ready, 1)
                if t + 2 < T_TILES:
                    skip_rows(t + 2)

        @block.vector
        def _(dve):
            v = nc.vector
            steps = [0]

            def then(ins):
                ins.then_inc(dve_step, 1)
                steps[0] += 1
                dve.wait_ge(dve_step, steps[0])

            def rsqrt(var, root, r, a):
                then(v.reciprocal(r, root))
                then(v.tensor_tensor(a, r, r, ALU.mult))
                then(v.tensor_tensor(a, a, var, ALU.mult))
                then(v.tensor_scalar(a, a, -0.5, 1.5, ALU.mult, ALU.add))
                then(v.tensor_tensor(r, r, a, ALU.mult))

            dve.wait_ge(zeroed, 1)
            for half in range(2):
                cols = slice(0, 5) if half == 0 else slice(5, 9)
                for c in (1, 2, 3, 4, 0) if half == 0 else range(5, 9):
                    dve.wait_ge(x_loaded[c], 16)
                    rows = META if c == 0 else P
                    part = xmeta if c == 0 else xin[:, c - 1, :]
                    v.bn_stats(stats[0:rows, c, 0, :], part[:, 0:HALF]).then_inc(dve_step, 1)
                    v.bn_stats(stats[0:rows, c, 1, :], part[:, HALF:D]).then_inc(dve_step, 1)
                    steps[0] += 2
                    dve.wait_ge(dve_step, steps[0])
                    then(v.bn_aggr(mv[0:rows, c, :], stats[0:rows, c, :, :]))
                v.tensor_scalar(mv[:, cols, 1], mv[:, cols, 1], LN_EPS, None, ALU.add).then_inc(var_ready, 1)
                dve.wait_ge(root_ready, half + 1)
                rsqrt(mv[:, cols, 1], small[:, 0, cols], rstd[:, cols], small[:, 1, cols])
                v.scalar_tensor_tensor(nmr[:, cols], mv[:, cols, 0], -1.0, rstd[:, cols], ALU.mult, ALU.mult)\
                    .then_inc(rstd_ready, 1)
            dve.wait_ge(params_turned, 1)
            then(v.tensor_copy(params[:], PS[:, 7, 0:N_ROWS]))
            for n in range(2 * KC):
                k = n % KC
                dve.wait_ge(z_turned, n + 1)
                if n >= 4:
                    dve.wait_ge(h_lo_ready, n - 3)
                v.tensor_scalar(hf[:, n % 4, :], PS[:, 3 + n % 4, :], column(ROW_G0 + k), column(ROW_B0 + k),
                                ALU.mult, ALU.add).then_inc(hf_ready, 1)
                if n == KC:
                    split_lo(dve, 0, 0, None)
            dve.wait_ge(z_turned, 2 * KC + 1)
            zm = PS[:, 7, P:2 * P].rearrange("p (k m) -> p k m", m=META)
            gain = params[:, ROW_G0:ROW_G0 + KC].unsqueeze(2).to_broadcast([P, KC, META])
            bias = params[:, ROW_B0:ROW_B0 + KC].unsqueeze(2).to_broadcast([P, KC, META])
            then(v.tensor_tensor(hfm, zm, gain, ALU.mult))
            v.tensor_tensor(hfm, hfm, bias, ALU.add).then_inc(hf_ready, 1)

            dve.wait_ge(sinks_loaded, 16)
            for e in range(2):
                rows = slice(64 * e, 64 * e + 64)
                then(v.tensor_copy(sink[rows, :].rearrange("p (c g) -> p c g", c=2),
                                   all_sinks[rows, :].rearrange("p (g c e) -> p c g e", g=2, c=2)[:, :, :, e]))
            then(v.tensor_scalar(neg_sink[:], sink[:], -1.0, None, ALU.mult))

            split_lo(dve, 1, 1, None)
            split_next(dve, split_lo, KV, 0, 1, 3)
            with dve.Fori(0, 2) as i:
                for n in range(2):
                    split_next(dve, split_lo, Q, i, n, 2 * n)
            for n in range(4):
                dve.wait_ge(v_turned, n + 1)
                v.tensor_copy(v_win[:, 4 * n:4 * n + 4, :],
                              PS[:, 3 + n, :].rearrange("p (w c) -> p w c", w=4)).then_inc(v_win_ready, 1)
            dve.wait_ge(v_turned, 5)
            v.tensor_copy(v_meta_bd[:], PS[0:2 * META, 7, 0:P]).then_inc(v_meta_ready, 1)

            def softmax_max(i, n, first=False):
                chunk = i * 4 + n
                dve.wait_ge(scores_done, chunk + 1)
                if first:
                    for g in range(2):
                        before = slice(WIN_COLS[g].start, WIN_COLS[g].start + CHUNK)
                        then(v.memset(S_PS[:, :, before], NEG_INF / SCALE))
                then_loop(i, v.tensor_reduce(row_max.rearrange("p (c g) -> p c g", c=2),
                                             S_PS.rearrange("p c (g k) -> p c g k", g=2), AX_X, ALU.max))
                wait(dve, sink_e_ready, chunk)
                v.scalar_tensor_tensor(neg_m, row_max, -SCALE, neg_sink[:], ALU.mult, ALU.min)\
                    .then_inc(neg_m_ready, 1)
                dve.wait_ge(neg_m_ready, chunk + 1)
                v.tensor_tensor(sink_m, neg_m, sink[:], ALU.add).then_inc(sink_m_ready, 1)

            def then_loop(turn, ins):
                ins.then_inc(conv_step, 1)
                loop_steps[0] += 1
                dve.wait_ge(conv_step, turn * STEPS + loop_steps[0])

            def scale_probs(i, n):
                chunk = i * 4 + n
                dve.wait_ge(probs_ready, chunk * 4 + 4)
                dve.wait_ge(sink_e_ready, chunk + 1)
                then_loop(i, v.tensor_tensor(denom, row_sum, sink_e, ALU.add))
                then_loop(i, v.reciprocal(r_den, denom))
                p4 = probs[:].rearrange("p c (g k) -> p (c g) k", g=2)
                v.tensor_tensor(p4, p4, r_den.unsqueeze(2).to_broadcast([P, 4, KEYS]), ALU.mult)\
                    .then_inc(probs_scaled, 1)

            def copy_pT(i, n):
                chunk = i * 4 + n
                dve.wait_ge(probs_turned, chunk + 1)
                wait(dve, o_done, chunk)
                v.tensor_copy(pT[:], PT_PS).then_inc(pT_ready, 1)

            def copy_o(i, n):
                chunk = i * 4 + n
                dve.wait_ge(o_done, chunk + 1)
                v.tensor_copy(q_o[:, :, bass.ds(chunk * CHUNK, CHUNK)], O_PS).then_inc(o_ready, 1)

            STEPS = 4 * 3 + 2
            loop_steps = [0]

            def mix_turn(i, first=False):
                loop_steps[0] = 0
                softmax_max(i, 0, first)
                for g in range(11):
                    tile, c = min(g // 3, 3), g - 3 * min(g // 3, 3)
                    if c == 0:
                        split_next(dve, split_lo, MIX, i, tile, g)
                    if tile == 2:
                        a, b = WITH_META[c]
                        dve.wait_ge(bank_read[MIX.banks[3 + c]], MIX.used(i, 3 + c) + 1)
                        dve.wait_ge(groups_done, MIX.groups(i, g) + 1)
                        v.tensor_tensor(u_sb[:, a:b], PS[:, MIX.banks[g], 0:b - a], ac_sb[:, a:b], ALU.mult)\
                            .then_inc(bank_read[MIX.banks[g]], 1)
                        if c == 2:
                            for j in range(3):
                                dve.wait_ge(bank_read[MIX.banks[6 + j]], MIX.used(i, 6 + j) + 1)
                            dst = conv_out[:, bass.ds(i, 1), :]
                            u3 = u_sb[:].unsqueeze(1)
                            tap = [params[:, bass.ds(i + (ROW_CONV + 4 * j), 1)] for j in range(3)]
                            then_loop(i, v.tensor_scalar(dst, u3[:, :, META:TOK], tap[2], None, ALU.mult))
                            for back in (1, 2):
                                ins = v.scalar_tensor_tensor(dst, u3[:, :, META - back:TOK - back],
                                                             tap[2 - back], dst, ALU.mult, ALU.add)
                                if back == 1:
                                    then_loop(i, ins)
                                else:
                                    ins.then_inc(conv_ready, 1)
                    if tile == 3:
                        dve.wait_ge(groups_done, MIX.groups(i, g) + 1)
                        dve.wait_ge(conv_ready, i + 1)
                        dst = conv_out[:, bass.ds(i, 1), HALF * c:HALF * c + HALF]
                        v.tensor_tensor(dst, PS[:, MIX.banks[g]:MIX.banks[g] + 1, :], dst, ALU.mult)\
                            .then_inc(bank_read[MIX.banks[g]], 1)
                    if g in TIMES_V_AFTER:
                        copy_o(i, TIMES_V_AFTER.index(g))
                    if g in TURN_AFTER:
                        copy_pT(i, TURN_AFTER.index(g))
                    if g + 1 in TURN_AFTER:
                        scale_probs(i, TURN_AFTER.index(g + 1))
                    if g in SCORES_AFTER:
                        softmax_max(i, SCORES_AFTER.index(g))
                assert loop_steps[0] == STEPS, loop_steps

            mix_turn(0, first=True)
            with dve.Fori(1, 4) as i:
                mix_turn(i)

            for n in range(8):
                i, c = n // 2, n % 2
                dve.wait_ge(groups_done, MAP.groups(0, n) + 1)
                v.tensor_scalar(pooled[:, i, HALF * c:HALF * c + HALF], PS[:, MAP.banks[n], :],
                                column(ROW_PS + i), None, ALU.mult).then_inc(bank_read[MAP.banks[n]], 1)

            for b in range(4):
                dve.wait_ge(bank_read[b], MAP.used_end[b])
            dve.wait_ge(o_ready, N_CHUNKS)
            for b, mixed in enumerate((conv_out, q_o, pooled)):
                def z_turn(i):
                    for n in range(2):
                        split_next(dve, split_lo, Z[b], i, n, 2 * n)
                        k = i * 2 + n
                        for c in range(2):
                            g = 2 * n + c
                            dve.wait_ge(bank_read[Z[b].banks[g]], Z[b].used(i, g) + 1)
                            wait(dve, y_hi_ready, k * 2 + (8 * b))
                            wait(dve, y_lo_ready, k * 2 + (8 * b))
                            v.tensor_tensor(y_f[:, bass.ds(c, 1), :], silu[:, bass.ds(c, 1), :],
                                            mixed[:, bass.ds(k, 1), HALF * c:HALF * c + HALF], ALU.mult)\
                                .then_inc(y_f_ready, 1)
                        for c in range(2):
                            dve.wait_ge(y_f_ready, k * 2 + (8 * b + c + 1))
                            dve.wait_ge(y_hi_ready, k * 2 + (8 * b + c + 1))
                            cols = slice(HALF * c, HALF * c + HALF)
                            v.tensor_tensor(y_lo[:, bass.ds(k, 1), cols], y_f[:, bass.ds(c, 1), :],
                                            y_hi[:, bass.ds(k, 1), cols].bitcast(F32), ALU.subtract)\
                                .then_inc(y_lo_ready, 1)
                def gate_turn(i):
                    for pair in range(2):
                        for n in range(2):
                            split_next(dve, split_lo, GATE[b], i, 3 * pair + n, 8 * pair + 2 * n)
                        if not (b == N_BRANCH - 1 and isinstance(i, int) and i == 1 and pair == 1):
                            split_next(dve, split_lo, GATE[b], i, 3 * pair + 2, 8 * pair + 4)
                        for n in range(2):
                            for c in range(2):
                                g, gate = 8 * pair + 4 + 2 * n + c, 8 * pair + 2 * n + c
                                bank, cols = GATE[b].banks[g], slice(HALF * c, HALF * c + HALF)
                                out_at = merged[:, bass.ds(i * 4 + (2 * pair + n), 1), cols]
                                prod = sig[:, n:n + 1, cols]
                                dve.wait_ge(groups_done, GATE[b].groups(i, g) + 1)
                                dve.wait_ge(bank_read[GATE[b].banks[gate]], GATE[b].used(i, gate) + 1)
                                v.tensor_tensor(prod, PS[:, bank:bank + 1, :], prod, ALU.mult)\
                                    .then_inc(bank_read[bank], 1)
                                dve.wait_ge(bank_read[bank], GATE[b].used(i, g) + 1)
                                if b == 0:
                                    v.tensor_copy(out_at, prod).then_inc(merged_step, 1)
                                else:
                                    v.tensor_tensor(out_at, out_at, prod, ALU.add).then_inc(merged_step, 1)

                two_turns(dve, z_turn, apart=b == 0)
                wait(dve, merged_step, 16 * b)
                two_turns(dve, gate_turn, apart=b != 1)

            dve.wait_ge(merged_step, 16 * N_BRANCH)
            for kind, n in OUT_SPLITS:
                if kind == "w":
                    split_out_lo(dve, n)
                else:
                    cols = slice(META + P * n, META + P * n + P)
                    dve.wait_ge(m_hi_ready, n + 1)
                    v.tensor_tensor(h_lo[:, :, cols], merged[:, :, P * n:P * n + P],
                                    h_hi[:, :, cols].bitcast(F32), ALU.subtract).then_inc(m_lo_ready, 1)

            def finish(t):
                dve.wait_ge(norm_ready, t + 1)
                then(v.tensor_tensor(res[:, t % 2, :], res[:, t % 2, :], gain1, ALU.mult))
                v.tensor_tensor(res[:, t % 2, :], res[:, t % 2, :], bias1, ALU.add).then_inc(row_ready, 1)

            dve.wait_ge(rows_loaded, 64)
            for t in range(T_TILES):
                dve.wait_ge(skip_ready, t + 1)
                if t >= 2:
                    dve.wait_ge(stored[t % 2], 16 * (t // 2))
                for h in range(2):
                    dve.wait_ge(out_done, out_count(t, h))
                    cols = slice(HALF * h, HALF * h + HALF)
                    v.tensor_tensor(res[:, t % 2, cols], PS[:, 2 * (t % 4) + h, :], hz[:, t % 2, cols],
                                    ALU.add).then_inc(res_half, 1)
                    dve.wait_ge(res_half, 2 * t + h + 1)
                    then(v.bn_stats(stats2[:, t, h, :], res[:, t % 2, cols]))
                then(v.bn_aggr(mv2[:, t, :], stats2[:, t, :, :]))
                var, root, r, a, nm = (small2[:, n, t:t + 1] for n in range(5))
                v.tensor_scalar(var, mv2[:, t, 1:2], LN_EPS, None, ALU.add).then_inc(var2_ready, 1)
                dve.wait_ge(var2_ready, t + 1)
                dve.wait_ge(root2_ready, t + 1)
                rsqrt(var, root, r, a)
                v.scalar_tensor_tensor(nm, mv2[:, t, 0:1], -1.0, r, ALU.mult, ALU.mult)\
                    .then_inc(rstd2_ready, 1)
                if t >= 1:
                    finish(t - 1)
            finish(T_TILES - 1)

        @block.tensor
        def _(pe):
            mm = nc.tensor.matmul
            turn = nc.tensor.transpose

            pe.wait_ge(ident_ready, 2)
            pe.wait_ge(params_loaded, 16 * 5)
            turn(PS[:, 7, 0:N_ROWS], prow, ident[0:N_ROWS, 0:N_ROWS]).then_inc(params_turned, 1)
            for n in range(2 * KC):
                half, k = n // KC, n % KC
                pe.wait_ge(z_ready, 4 if half == 0 else 9)
                if n >= 4:
                    pe.wait_ge(hf_ready, n - 3)
                for t in range(4):
                    last = turn(PS[:, 3 + n % 4, P * t:P * t + P], xin[:, 4 * half + t, P * k:P * k + P],
                                ident[:])
                last.then_inc(z_turned, 1)
            for k in range(KC):
                last = turn(PS[:, 7, P + META * k:P + META * k + META], xmeta[:, P * k:P * k + P],
                            ident[0:META, 0:META])
            last.then_inc(z_turned, 1)

            def three_passes(dst, w_parts, x_parts, n_k, begin=True, end=True):
                (wh, wl), (xh, xl) = w_parts, x_parts
                for k in range(n_k):
                    for p, (a, b) in enumerate(((wh, xh), (wh, xl), (wl, xh))):
                        last = mm(dst, a(k), b(k), start=begin and k == 0 and p == 0,
                                  stop=end and k == n_k - 1 and p == 2)
                return last

            def project(sec, i, g, slot, tokens, more=0):
                b = sec.banks[g]
                a, z = tokens
                wait(pe, bank_read[b], sec.used(i, g) + more)
                three_passes(PS[:, b, 0:z - a],
                             (lambda k: w_hi[:, slot, k, :], lambda k: w_lo[:, slot, k, :]),
                             (lambda k: h_hi[:, k, a:z], lambda k: h_lo[:, k, a:z]), KC)\
                    .then_inc(groups_done, 1)

            pe.wait_ge(h_lo_ready, 2 * KC + 1)
            for n in range(2):
                pe.wait_ge(w_lo_ready, KV.tile(0, n) + 1)
                for c in range(3):
                    project(KV, 0, 3 * n + c, n, WITH_META[c])
            with pe.Fori(0, 2) as i:
                for n in range(2):
                    pe.wait_ge(w_lo_ready, Q.tile(i, n) + 1)
                    for c in range(2):
                        project(Q, i, 2 * n + c, n, REAL_ONLY[c])

            for b in range(3):
                pe.wait_ge(bank_read[b], KV.used_end[b])
            pe.wait_ge(zeroed, N_ZEROED)
            for c in range(N_CHUNKS):
                last = turn(PS[:, 3 + c // 4, P * (c % 4):P * (c % 4) + P],
                            vT[:, META + CHUNK * c:META + CHUNK * c + P], ident[:])
                if c % 4 == 3:
                    last.then_inc(v_turned, 1)
            pe.wait_ge(meta_staged, 4)
            turn(PS[0:2 * META, 7, 0:P], vT_meta_bd[:], ident[:]).then_inc(v_turned, 1)
            pe.wait_ge(v_win_ready, 2)

            def scores(i, n):
                chunk = i * 4 + n
                pe.wait_ge(qk_staged, chunk * 3 + 3)
                wait(pe, probs_ready, chunk * 4)
                for c in range(2):
                    last = mm(S_PS[:, c, :], q_stage[:, 2 * c:2 * c + 2, :].rearrange("p t q -> p (t q)"),
                              k_stage[:], start=True, stop=True)
                last.then_inc(scores_done, 1)

            def turn_probs(i, n):
                chunk = i * 4 + n
                pe.wait_ge(probs_scaled, chunk + 1)
                wait(pe, pT_ready, chunk)
                wait(pe, pT_meta_ready, chunk)
                for c in range(2):
                    for g in range(2):
                        turn(PT_PS[:, g, c, :], probs[:, c, WIN_COLS[g]], ident[:])
                    last = turn(PTM_PS[:, c, :], probs[:, c, META_COLS], ident[:])
                last.then_inc(probs_turned, 1)

            def times_v(i, n):
                chunk = i * 4 + n
                pe.wait_ge(v_staged, chunk + 1)
                pe.wait_ge(pT_ready, chunk + 1)
                pe.wait_ge(pT_meta_ready, chunk + 1)
                wait(pe, o_ready, chunk)
                out_at = PS[:, 7, 0:4 * CHUNK]
                mm(out_at, v_meta_bd[:], pT_meta[:].rearrange("p c r -> p (c r)"), start=True, stop=False)
                for g in range(2):
                    last = mm(out_at, v_stage[:, g:g + 2, :].rearrange("p z d -> p (z d)"),
                              pT[:, g, :, :].rearrange("p c r -> p (c r)"), start=False, stop=g == 1)
                last.then_inc(o_done, 1)

            def mix_turn(i, first=False):
                scores(i, 0)
                for g in range(11):
                    tile, c = min(g // 3, 3), g - 3 * min(g // 3, 3)
                    if c == 0:
                        pe.wait_ge(w_lo_ready, MIX.tile(i, tile) + 1)
                    project(MIX, i, g, tile % 2, (WITH_META if tile < 3 else REAL_ONLY)[c])
                    if g in TIMES_V_AFTER:
                        times_v(i, TIMES_V_AFTER.index(g))
                    if g in TURN_AFTER:
                        if first and g == TURN_AFTER[0]:
                            pe.wait_ge(v_win_ready, 4)
                            pe.wait_ge(v_meta_ready, 1)
                        turn_probs(i, TURN_AFTER.index(g))
                    if g in SCORES_AFTER:
                        scores(i, SCORES_AFTER.index(g))

            mix_turn(0, first=True)
            with pe.Fori(1, 4) as i:
                mix_turn(i)

            pe.wait_ge(pool_w_loaded, 16)
            pe.wait_ge(pooled_ready, 4)
            pe.wait_ge(probs_ready, 4 * N_CHUNKS)
            for n in range(8):
                g, c = n // 2, n % 2
                pe.wait_ge(bank_read[MAP.banks[n]], MAP.used(0, n))
                mm(PS[:, MAP.banks[n], :], pool_wt[:, g, :], pooled[:, g, HALF * c:HALF * c + HALF],
                   start=True, stop=True).then_inc(groups_done, 1)

            with pe.Fori(0, N_BRANCH) as b:
                with pe.Fori(0, 2) as i:
                    for n in range(2):
                        pe.wait_ge(w_lo_ready, b * BRANCH_TILES + Z[0].tile(i, n) + 1)
                        for c in range(2):
                            project(Z[0], i, 2 * n + c, n, REAL_ONLY[c], more=b * BRANCH_USES)
                with pe.Fori(0, 2) as i:
                    for pair in range(2):
                        for n in range(2):
                            tile = 3 * pair + n
                            pe.wait_ge(w_lo_ready, b * BRANCH_TILES + GATE[0].tile(i, tile) + 1)
                            for c in range(2):
                                project(GATE[0], i, 8 * pair + 2 * n + c, tile % 2, REAL_ONLY[c],
                                        more=b * BRANCH_USES)
                        tile = 3 * pair + 2
                        pe.wait_ge(w_lo_ready, b * BRANCH_TILES + GATE[0].tile(i, tile) + 1)
                        pe.wait_ge(y_lo_ready, b * 8 + 8)
                        wh, wl = (w[:, tile % 2, :, :].rearrange("p (k two) c -> p k (two c)", two=2)
                                  for w in (w_hi, w_lo))
                        for n in range(2):
                            for c in range(2):
                                g = 8 * pair + 4 + 2 * n + c
                                bank = GATE[0].banks[g]
                                pe.wait_ge(bank_read[bank], GATE[0].used(i, g) + b * BRANCH_USES)
                                three_passes(PS[:, bank, :],
                                             (lambda k: wh[:, k, P * n:P * n + P],
                                              lambda k: wl[:, k, P * n:P * n + P]),
                                             (lambda k: y_hi[:, k, HALF * c:HALF * c + HALF],
                                              lambda k: y_lo[:, k, HALF * c:HALF * c + HALF]), 4)\
                                    .then_inc(groups_done, 1)

            def out_rows_product(t, h, k0, k1):
                tokens = slice(META + P * t, META + P * t + P)
                return three_passes(PS[:, 2 * (t % 4) + h, :],
                                    (lambda k: h_hi[:, k0 + k, tokens], lambda k: h_lo[:, k0 + k, tokens]),
                                    (lambda k: wo_hi[h][:, k0 + k, :], lambda k: wo_lo[h][:, k0 + k, :]),
                                    k1 - k0, begin=k0 == 0, end=k1 == KC)

            for n in range(OUT_PIECES):
                h, k = n // 4, 2 * (n % 4)
                pe.wait_ge(wo_lo_ready, n + 1)
                for t in range(4):
                    if n == 0:
                        pe.wait_ge(m_lo_ready, t + 1)
                    last = out_rows_product(t, h, k, k + 2)
                    if k == KC - 2:
                        last.then_inc(out_done, 1)
            for t in range(4, T_TILES):
                pe.wait_ge(m_lo_ready, t + 1)
                for h in range(2):
                    pe.wait_ge(res_half, 2 * (t - 4) + h + 1)
                    out_rows_product(t, h, 0, KC).then_inc(out_done, 1)


_INS = ['x', 'meta_tokens', 'ln0_g', 'ln0_b', 'w_in', 'b_gate', 'conv_w', 'attn_sinks', 'pool_w', 'pool_scale',
        'w_br_a', 'w_br_b', 'w_br_c', 'w_out', 'ln_g', 'ln_b']
_OUTS = [((1, 1024, 1024), 'float32')]


def kernel(**inputs):
    import numpy as _np
    import concourse.bacc as _bacc
    from concourse import mybir as _mybir
    from concourse.bass_utils import run_bass_kernel_spmd as _run

    nc = _bacc.Bacc("TRN2", target_bir_lowering=False, num_devices=1)
    arrays, args = {}, []
    for name in _INS:
        a = _np.ascontiguousarray(inputs[name])
        arrays[f"in_{name}_dram"] = a
        args.append(nc.dram_tensor(f"in_{name}_dram", a.shape, _mybir.dt.from_np(a.dtype), kind="ExternalInput").ap())
    for i, (shape, dtype) in enumerate(_OUTS):
        dt = _mybir.dt.from_np(_np.dtype(dtype))
        args.append(nc.dram_tensor(f"out_{i}_dram", shape, dt, kind="ExternalOutput").ap())
    hybrid_layer(nc, *args)
    r = _run(nc, [arrays], core_ids=[0])
    return r.results[0]["out_0_dram"]
```

```python
from contextlib import ExitStack

import concourse.bass as bass
from concourse import mybir

F32 = mybir.dt.float32
F32R = mybir.dt.float32r
ALU = mybir.AluOpType
ACT = mybir.ActivationFunctionType
AX_X = mybir.AxisListType.X

P = 128
D = 1024
KC = D // P
SEQ = 1024
META = 16
TOK = META + SEQ
CHUNK = 64
N_CHUNKS = SEQ // CHUNK
HEAD = 64
PAD = CHUNK
KEYS = META + 2 * CHUNK
LN_EPS = 1e-5
NEG_INF = -1e30
ALPHA = 2 ** 0.25
SCALE = HEAD ** -0.5
POOL_WINDOWS = (2, 4, 8, 16)
N_BRANCH = 3
HALF = 512

COL_AB, COL_AC, COL_AH, COL_AZ = 0, 512, 1024, 1536
COL_Q, COL_K, COL_V, COL_BZ = 2048, 2560, 2688, 2816
COL_CU, COL_CZ, COL_GATE = 3328, 3840, 4352

WITH_META = ((0, 348), (348, 694), (694, TOK))
REAL_ONLY = ((META, META + HALF), (META + HALF, TOK))

SCORES_AFTER = (-1, 2, 5, 7)
TURN_AFTER = (1, 4, 7, 9)
TIMES_V_AFTER = (2, 5, 8, 10)
N_ZEROED = 6

HF_ON_DVE = (9, 11, 13, 15)
LO_ON_DVE = (3, 7, 9, 11, 13, 15)

ROW_G0, ROW_B0, ROW_BG, ROW_CONV, ROW_PS = 0, 8, 16, 40, 52
N_ROWS = 56


class Section:

    def __init__(self, before, banks, tiles, turns):
        self.tile0 = before.tile_end if before else 0
        self.group0 = before.group_end if before else 0
        self.used0 = list(before.used_end) if before else [0] * 4
        self.banks, self.tiles, self.turns = banks, tiles, turns
        self.per_turn = [banks.count(b) for b in range(4)]
        self.tile_end = self.tile0 + tiles * turns
        self.group_end = self.group0 + len(banks) * turns
        self.used_end = [u + n * turns for u, n in zip(self.used0, self.per_turn)]

    def tile(self, turn, n):
        return turn * self.tiles + (self.tile0 + n)

    def groups(self, turn, g):
        return turn * len(self.banks) + (self.group0 + g)

    def used(self, turn, g):
        b = self.banks[g]
        return turn * self.per_turn[b] + (self.used0[b] + self.banks[:g].count(b))


def wait(eng, sem, value):
    if not isinstance(value, int) or value > 0:
        eng.wait_ge(sem, value)


def hybrid_layer(nc, x, meta_tokens, ln0_g, ln0_b, w_in, b_gate, conv_w, attn_sinks, pool_w, pool_scale,
                 w_br_a, w_br_b, w_br_c, w_out, ln_g, ln_b, out):
    Q = Section(None, (0, 1, 2, 1), 2, 2)
    KV = Section(Q, (0, 1, 2, 0, 1, 2), 2, 1)
    MIX = Section(KV, (0, 1, 2, 0, 1, 2, 0, 1, 2, 0, 1), 4, 4)
    MAP = Section(MIX, (0, 1, 2, 3, 0, 1, 2, 3), 0, 1)
    Z, GATE = [], []
    last = MAP
    for _ in range(N_BRANCH):
        Z.append(Section(last, (0, 1, 2, 3), 2, 2))
        GATE.append(Section(Z[-1], (0, 1, 2, 3) * 4, 6, 2))
        last = GATE[-1]
    N_TILES = last.tile_end
    GROUPS_IN = last.group_end
    BRANCH_TILES = GATE[0].tile_end - Z[0].tile0
    BRANCH_GROUPS = GATE[0].group_end - Z[0].group0
    BRANCH_USES = GATE[0].used_end[0] - Z[0].used0[0]
    OUT_PIECES = 8
    H_LAST_GROUP = GROUPS_IN - 4
    T_TILES = SEQ // P
    SKIP_SLOTS = 4
    SIDE = 2

    with ExitStack() as ctx:
        def sb(name, shape, dt=F32, stack=ctx):
            return stack.enter_context(nc.sbuf_tensor(name, shape, dt))

        def sem(name):
            return ctx.enter_context(nc.semaphore(name))

        h_hi = sb("h_hi", [P, KC, TOK], F32R)
        h_lo = sb("h_lo", [P, KC, TOK], F32R)
        raw = sb("raw", [P, 2, KC, P])
        w_hi = sb("w_hi", [P, 2, KC, P], F32R)
        w_lo = sb("w_lo", [P, 2, KC, P], F32R)
        merged = sb("merged", [P, KC, SEQ])
        ident = sb("ident", [P, P])
        params = sb("params", [P, N_ROWS])
        rstd = sb("rstd", [P, 1 + T_TILES])
        nmr = sb("nmr", [P, 1 + T_TILES])
        gate_bias = sb("gate_bias", [P, 4])

        conv_out = merged[:, 0:4, :]
        xin = merged

        def column(row):
            return params[:, row:row + 1]

        qm = ExitStack()
        q_o = sb("q_o", [P, 4, SEQ], stack=qm)
        pooled = sb("pooled", [P, 4, SEQ], stack=qm)
        hf = q_o[:, :, 0:HALF]
        gain0 = pooled[:, 3, :]
        xmeta = pooled[0:META, 0, :]
        META_COL = T_TILES
        prow = pooled[0:N_ROWS, 1, 0:P]
        hfm = pooled[:, 2, 0:P].rearrange("p (k m) -> p k m", m=META)

        one = ExitStack()
        kT = sb("kT", [P, META + PAD + SEQ], stack=one)
        vT = sb("vT", [P, META + PAD + SEQ], stack=one)
        v_win = sb("v_win", [P, N_CHUNKS, P], stack=one)
        v_meta_bd = sb("v_meta_bd", [2 * META, P], stack=one)
        vT_meta_bd = sb("vT_meta_bd", [P, 2 * META], stack=one)
        q_stage = sb("q_stage", [P, 4, CHUNK], stack=one)
        k_stage = sb("k_stage", [P, 2 * KEYS], stack=one)
        v_stage = sb("v_stage", [P, 3, HEAD], stack=one)
        probs = sb("probs", [P, 2, 2 * KEYS], stack=one)
        pT = sb("pT", [P, 2, 2, P], stack=one)
        pT_meta = sb("pT_meta", [2 * META, 2, P], stack=one)
        ac_sb = sb("ac_sb", [P, TOK], stack=one)
        u_sb = sb("u_sb", [P, TOK], stack=one)
        cu_sb = sb("cu_sb", [P, TOK], stack=one)
        win_a = sb("win_a", [P, TOK], stack=one)
        win_b = sb("win_b", [P, TOK], stack=one)
        bias0 = win_a[:, 0:D]
        pool_wt = sb("pool_wt", [P, 4, P], stack=one)
        small = sb("small", [P, 8, 16], stack=one)
        stats = sb("stats", [P, 1 + T_TILES, 2, 6], stack=one)
        mv = sb("mv", [P, 1 + T_TILES, 2], stack=one)
        neg_sink = sb("neg_sink", [P, 4], stack=one)
        sink = sb("sink", [P, 4], stack=one)
        all_sinks = sb("all_sinks", [P, 8], stack=one)
        one.close()
        row_max, neg_m, sink_m, sink_e = (small[:, n, 0:4] for n in range(4))
        row_sum, denom, r_den = (small[:, n, 0:4] for n in range(4, 7))

        two = ExitStack()
        y_hi = sb("y_hi", [P, 4, SEQ], F32R, stack=two)
        y_lo = sb("y_lo", [P, 4, SEQ], F32R, stack=two)
        silu = sb("silu", [P, 2, HALF], stack=two)
        y_f = sb("y_f", [P, 2, HALF], stack=two)
        sig = sb("sig", [P, 2, SEQ], stack=two)
        two.close()
        qm.close()

        three = ExitStack()
        wo_hi0 = sb("wo_hi0", [P, KC, HALF], F32R, stack=three)
        wo_lo0 = sb("wo_lo0", [P, KC, HALF], F32R, stack=three)
        wo_hi1 = sb("wo_hi1", [P, KC, HALF], F32R, stack=three)
        wo_lo1 = sb("wo_lo1", [P, KC, HALF], F32R, stack=three)
        skip = sb("skip", [P, SKIP_SLOTS, D], stack=three)
        stats2 = sb("stats2", [P, T_TILES, 2, 6], stack=three)
        mv2 = sb("mv2", [P, T_TILES, 2], stack=three)
        small2 = sb("small2", [P, 8, T_TILES], stack=three)
        three.close()
        wo_hi, wo_lo = (wo_hi0, wo_hi1), (wo_lo0, wo_lo1)
        gain1, bias1 = (merged[:, n, :] for n in range(2))
        res = merged[:, 2:4, :]
        skip_dram = nc.dram_tensor("skip_dram", (T_TILES, P, D), F32, kind="Internal").ap()

        PS = ctx.enter_context(nc.psum_tensor("PS", [P, 8, HALF], F32))
        S_PS = PS[:, 3:5, 0:2 * KEYS]
        PT_PS = PS[:, 5, :].rearrange("p (g c r) -> p g c r", g=2, c=2)
        PTM_PS = PS[0:2 * META, 6, 0:2 * P].rearrange("p (c r) -> p c r", c=2)
        O_PS = PS[:, 7, 0:4 * CHUNK].rearrange("p (t q) -> p t q", t=4)
        META_COLS = slice(2 * CHUNK, 2 * CHUNK + 2 * META)
        WIN_COLS = (slice(0, 2 * CHUNK), slice(KEYS + META, 2 * KEYS))

        x_loaded = [sem(f"x_loaded{n}") for n in range(1 + T_TILES)]
        params_loaded = sem("params_loaded")
        sinks_loaded = sem("sinks_loaded")
        pool_w_loaded = sem("pool_w_loaded")
        raw_loaded = [sem(f"raw_loaded{s}") for s in range(2)]
        ident_ready = sem("ident_ready")
        zeroed = sem("zeroed")
        params_turned = sem("params_turned")
        params_ready = sem("params_ready")
        dve_step = sem("dve_step")
        var_ready = sem("var_ready")
        root_ready = sem("root_ready")
        rstd_ready = sem("rstd_ready")
        z_by_act = sem("z_by_act")
        z_by_dve = sem("z_by_dve")
        z_turned = sem("z_turned")
        hf_by_act = sem("hf_by_act")
        hf_by_dve = sem("hf_by_dve")
        hfm_ready = sem("hfm_ready")
        h_hi_ready = sem("h_hi_ready")
        h_lo_by_pool = sem("h_lo_by_pool")
        h_lo_by_dve = sem("h_lo_by_dve")
        meta_lo_ready = sem("meta_lo_ready")
        w_hi_ready = sem("w_hi_ready")
        w_lo_ready = sem("w_lo_ready")
        groups_done = sem("groups_done")
        bank_read = [sem(f"bank_read{b}") for b in range(4)]
        v_turned = sem("v_turned")
        v_win_ready = sem("v_win_ready")
        v_meta_ready = sem("v_meta_ready")
        meta_staged = sem("meta_staged")
        qk_staged = sem("qk_staged")
        v_staged = sem("v_staged")
        scores_done = sem("scores_done")
        neg_m_ready = sem("neg_m_ready")
        sink_m_ready = sem("sink_m_ready")
        probs_ready = sem("probs_ready")
        sink_e_ready = sem("sink_e_ready")
        probs_scaled = sem("probs_scaled")
        probs_turned = sem("probs_turned")
        pT_ready = sem("pT_ready")
        pT_meta_ready = sem("pT_meta_ready")
        o_done = sem("o_done")
        o_ready = sem("o_ready")
        conv_ready = sem("conv_ready")
        conv_step = sem("conv_step")
        pool_step = sem("pool_step")
        pooled_ready = sem("pooled_ready")
        y_f_ready = sem("y_f_ready")
        gate_bias_ready = sem("gate_bias_ready")
        y_hi_ready = sem("y_hi_ready")
        y_lo_ready = sem("y_lo_ready")
        merged_step = sem("merged_step")
        m_hi_ready = sem("m_hi_ready")
        m_lo_ready = sem("m_lo_ready")
        wo_hi_ready = sem("wo_hi_ready")
        wo_lo_ready = sem("wo_lo_ready")
        rows0_loaded = sem("rows0_loaded")
        rows1_loaded = sem("rows1_loaded")
        rows0_scaled = sem("rows0_scaled")
        skip_step = sem("skip_step")
        skip_ready = sem("skip_ready")
        skip_stored = sem("skip_stored")
        skip_loaded = [sem(f"skip_loaded{s}") for s in range(SKIP_SLOTS)]
        out_done = sem("out_done")
        res_half = sem("res_half")
        var2_ready = sem("var2_ready")
        root2_ready = sem("root2_ready")
        rstd2_ready = sem("rstd2_ready")
        tail_step = sem("tail_step")
        row_ready = sem("row_ready")
        stored = [sem(f"stored{s}") for s in range(2)]

        def wait_hf(eng, n):
            if n in HF_ON_DVE:
                eng.wait_ge(hf_by_dve, HF_ON_DVE.index(n) + 1)
            else:
                eng.wait_ge(hf_by_act, n + 1 - sum(m < n for m in HF_ON_DVE))

        def wait_lo(eng, n):
            if n in LO_ON_DVE:
                eng.wait_ge(h_lo_by_dve, LO_ON_DVE.index(n) + 1)
            else:
                eng.wait_ge(h_lo_by_pool, n + 1 - sum(m < n for m in LO_ON_DVE))

        def wait_h_half(eng, half):
            for n in (KC * half + KC - 2, KC * half + KC - 1):
                wait_lo(eng, n)

        def block_cols(n):
            return slice(META + HALF * (n // KC), META + HALF * (n // KC) + HALF)

        def two_turns(eng, body, apart):
            if apart:
                body(0)
                body(1)
            else:
                with eng.Fori(0, 2) as i:
                    body(i)

        block = ctx.enter_context(nc.Block())

        w_view = w_in[0].rearrange("(k p) n -> p k n", p=P)

        def token_col(t):
            return t if t < META else t + PAD

        def kv_parts(a, b):
            if a < META:
                return ((0, META - a, token_col(a)), (META - a, b - a, token_col(META)))
            return ((0, b - a, token_col(a)),)

        @block.sync
        def _(sp):
            x_rows = x[0].rearrange("(t p) d -> t p d", p=P)
            for t in range(4):
                sp.dma_start(xin[:, t, :], x_rows[t]).then_inc(x_loaded[t], 16)
            for row, src in ((ROW_G0, ln0_g.rearrange("(r c) -> r c", c=P)),
                             (ROW_B0, ln0_b.rearrange("(r c) -> r c", c=P)),
                             (ROW_BG, b_gate[0].rearrange("(r c) -> r c", c=P)),
                             (ROW_CONV, conv_w[0].rearrange("j (r c) -> (j r) c", c=P)),
                             (ROW_PS, pool_scale[0].rearrange("(r c) -> r c", c=P))):
                sp.dma_start(prow[row:row + src.shape[0], :], src).then_inc(params_loaded, 16)

            def load_columns(tile, slot, col):
                raw_free(tile)
                for k in (4, 0):
                    sp.dma_start(raw[:, slot, k:k + 4, :], w_view[:, k:k + 4, bass.ds(col, P)])\
                        .then_inc(raw_loaded[slot], 16)

            def load_heads(tile, slot, col):
                raw_free(tile)
                for half in range(2):
                    sp.dma_start(raw[:, slot, :, HEAD * half:HEAD * (half + 1)],
                                 w_view[:, :, bass.ds(col + 256 * half, HEAD)])\
                        .then_inc(raw_loaded[slot], 16)

            def raw_free(tile):
                if isinstance(tile, int) and tile < 2:
                    return
                sp.wait_ge(w_hi_ready, tile - 1)
                sp.wait_ge(w_lo_ready, tile - 1)

            def load_q(i, n):
                load_heads(Q.tile(i, n), n, i * (2 * HEAD) + (COL_Q + HEAD * n))

            load_q(0, 0)
            for t in range(4, T_TILES):
                sp.dma_start(xin[:, t, :], x_rows[t]).then_inc(x_loaded[t], 16)
            load_q(0, 1)
            sp.dma_start(xmeta, meta_tokens).then_inc(x_loaded[META_COL], 16)
            for dst, src in ((gain0, ln0_g), (bias0, ln0_b)):
                sp.dma_start(dst, src.rearrange("(a n) -> a n", a=1).partition_broadcast(P))\
                    .then_inc(rows0_loaded, 16)
            sp.dma_start(all_sinks[:], attn_sinks[0:1, :].partition_broadcast(P)).then_inc(sinks_loaded, 16)
            sp.dma_start(pool_wt[:], pool_w[0].rearrange("g c d -> c g d")).then_inc(pool_w_loaded, 16)
            for n in range(2):
                load_q(1, n)
            load_columns(KV.tile(0, 0), 0, COL_K)
            load_columns(KV.tile(0, 1), 1, COL_V)

            def load_mix(i, keep_skip=False):
                for n, col in enumerate((COL_CU, COL_AC, COL_AH, COL_AB)):
                    load_columns(MIX.tile(i, n), n % 2, i * P + col)
                    if keep_skip and n in (1, 2):
                        for t in range(4 * n - 4, 4 * n):
                            sp.wait_ge(skip_ready, t + 1)
                            sp.dma_start(skip_dram[t], xin[:, t, :]).then_inc(skip_stored, 16)

            load_mix(0, keep_skip=True)
            with sp.Fori(1, 4) as i:
                load_mix(i)
            for b, (col_z, w_br) in enumerate(((COL_AZ, w_br_a), (COL_BZ, w_br_b), (COL_CZ, w_br_c))):
                with sp.Fori(0, 2) as i:
                    for n in range(2):
                        if b == 1:
                            load_heads(Z[b].tile(i, n), n, i * (2 * HEAD) + (col_z + HEAD * n))
                        else:
                            load_columns(Z[b].tile(i, n), n, i * (2 * P) + (col_z + P * n))
                with sp.Fori(0, 2) as i:
                    for pair in range(2):
                        for n in range(2):
                            tile = GATE[b].tile(i, 3 * pair + n)
                            load_columns(tile, (3 * pair + n) % 2,
                                         i * (4 * P) + (COL_GATE + D * b + P * (2 * pair + n)))
                        n = 3 * pair + 2
                        raw_free(GATE[b].tile(i, n))
                        dst = raw[:, n % 2, :, :].rearrange("p (k two) c -> p k (two c)", two=2)
                        for half in (1, 0):
                            rows = (w_br[0, 256 * half:256 * half + 256, :].rearrange("(k p) n -> p k n", p=64)
                                    if b == 1 else
                                    w_br[0].rearrange("(k p) n -> p k n", p=P)[64 * half:64 * half + 64])
                            sp.dma_start(dst[64 * half:64 * half + 64],
                                         rows[:, :, bass.ds(i * (4 * P) + 2 * P * pair, 2 * P)])\
                                .then_inc(raw_loaded[n % 2], 16)
            wo_view = w_out[0].rearrange("(k p) n -> p k n", p=P)
            for n in range(OUT_PIECES):
                half, k = n // 4, 2 * (n % 4)
                if n < 2:
                    raw_free(N_TILES + n)
                else:
                    sp.wait_ge(wo_hi_ready, n - 1)
                    sp.wait_ge(wo_lo_ready, n - 1)
                dst = raw[:, n % 2, :, :].rearrange("p (k four) c -> p k (four c)", four=4)
                for j in range(2):
                    sp.dma_start(dst[:, j, :], wo_view[:, k + j, HALF * half:HALF * half + HALF])\
                        .then_inc(raw_loaded[n % 2], 16)
            sp.wait_ge(m_hi_ready, 2 * KC)
            sp.wait_ge(m_lo_ready, 2 * KC)
            for dst, src in ((gain1, ln_g[0]), (bias1, ln_b[0])):
                sp.dma_start(dst, src.rearrange("(a n) -> a n", a=1).partition_broadcast(P))\
                    .then_inc(rows1_loaded, 16)
            out_rows = out[0].rearrange("(t p) d -> t p d", p=P)

            def load_skip(t):
                sp.dma_start(skip[:, t % SKIP_SLOTS, :], skip_dram[t])\
                    .then_inc(skip_loaded[t % SKIP_SLOTS], 16)

            sp.wait_ge(skip_stored, 16 * T_TILES)
            for t in range(SKIP_SLOTS):
                load_skip(t)
            for t in range(T_TILES):
                if t + SKIP_SLOTS < T_TILES:
                    sp.wait_ge(res_half, 2 * t + 2)
                    load_skip(t + SKIP_SLOTS)
                for part in ((0, D),) if t < T_TILES - 1 else ((0, HALF), (HALF, D)):
                    cols = slice(*part)
                    sp.wait_ge(row_ready, t + 1 + (part[0] > 0))
                    sp.dma_start(out_rows[t][:, cols], res[:, t % 2, cols]).then_inc(stored[t % 2], 16)
            for s in range(2):
                sp.wait_ge(stored[s], 16 * (T_TILES // 2 + s))

        @block.gpsimd
        def _(pool):
            g = nc.gpsimd
            g.memset(ident[:], 0.0).then_inc(ident_ready, 1)
            g.memset(mv[:], 1.0).then_inc(zeroed, 1)
            pool.wait_ge(ident_ready, 1)
            g.affine_select(out=ident[:], in_=ident[:], compare_op=ALU.not_equal, fill=1.0, base=0,
                            pattern=[[-1, P]], channel_multiplier=1).then_inc(ident_ready, 1)
            g.memset(kT[:, META:META + PAD], 0.0).then_inc(zeroed, 1)
            g.memset(vT[:, META:META + PAD], 0.0).then_inc(zeroed, 1)
            g.memset(k_stage[:], 0.0).then_inc(zeroed, 1)
            g.memset(v_stage[:], 0.0).then_inc(zeroed, 1)
            g.memset(vT_meta_bd[:], 0.0).then_inc(zeroed, 1)
            for n in range(2 * KC):
                if n not in LO_ON_DVE:
                    pool.wait_ge(h_hi_ready, n + 1)
                    cols = block_cols(n)
                    g.tensor_tensor(h_lo[:, n % KC, cols], hf[:, n % 4, :], h_hi[:, n % KC, cols].bitcast(F32),
                                    ALU.subtract).then_inc(h_lo_by_pool, 1)

            pool.wait_ge(rows0_scaled, 2)
            pool.wait_ge(z_turned, 2 * KC)
            for t in range(T_TILES):
                if t == 2:
                    pool.wait_ge(h_hi_ready, 2 * KC + 1)
                    g.tensor_tensor(h_lo[:, :, 0:META], hfm, h_hi[:, :, 0:META].bitcast(F32), ALU.subtract)\
                        .then_inc(meta_lo_ready, 1)
                g.tensor_tensor(xin[:, t, :], xin[:, t, :], gain0, ALU.mult).then_inc(skip_step, 1)
                pool.wait_ge(skip_step, t + 1)
                g.tensor_tensor(xin[:, t, :], xin[:, t, :], bias0, ALU.add).then_inc(skip_ready, 1)
            pool.wait_ge(skip_ready, T_TILES)

            step = 0
            for i, w in enumerate(POOL_WINDOWS):
                for n in range(3):
                    pool.wait_ge(bank_read[MIX.banks[n]], MIX.used(i, n) + 1)
                src, size = cu_sb, 1
                for dst in (win_a, win_b, win_a, win_b)[:i + 1]:
                    lead = 2 * size - 1
                    g.tensor_tensor(dst[:, lead:TOK], src[:, lead:TOK], src[:, lead - size:TOK - size],
                                    ALU.add).then_inc(pool_step, 1)
                    step += 1
                    pool.wait_ge(pool_step, step)
                    src, size = dst, 2 * size
                g.tensor_scalar(src[:, META:TOK], src[:, META:TOK], 1.0 / w, None, ALU.mult)\
                    .then_inc(pool_step, 1)
                step += 1
                pool.wait_ge(pool_step, step)
                g.tensor_tensor(pooled[:, i, :], src[:, META:TOK], cu_sb[:, META:TOK], ALU.subtract)\
                    .then_inc(pooled_ready, 1)

        def split_hi(act, tile, slot, groups_before):
            n = tile // 2 if isinstance(tile, int) else None
            act.wait_ge(raw_loaded[slot], raw_count(tile, slot))
            if groups_before is not None:
                act.wait_ge(groups_done, groups_before)
            nc.scalar.activation(w_hi[:, slot], raw[:, slot], ACT.Copy).then_inc(w_hi_ready, 1)

        def split_lo(dve, tile, slot, groups_before):
            dve.wait_ge(raw_loaded[slot], raw_count(tile, slot))
            dve.wait_ge(w_hi_ready, tile + 1)
            if groups_before is not None:
                dve.wait_ge(groups_done, groups_before)
            nc.vector.tensor_tensor(w_lo[:, slot], raw[:, slot], w_hi[:, slot].bitcast(F32),
                                    ALU.subtract).then_inc(w_lo_ready, 1)

        def raw_count(tile, slot):
            return tile * 16 + (32 - 16 * slot)

        def split_next(eng, split, sec, turn, n, g):
            split(eng, sec.tile(turn, n) + 1, (n + 1) % 2, sec.groups(turn, g))

        def out_part(parts, n):
            half, k = n // 4, 2 * (n % 4)
            return (parts[half][:, k:k + 2, :],
                    raw[:, n % 2, :, :].rearrange("p (k four) c -> p k (four c)", four=4))

        def split_out_hi(act, n):
            act.wait_ge(raw_loaded[n % 2], raw_count(N_TILES + n, n % 2))
            dst, src = out_part(wo_hi, n)
            nc.scalar.activation(dst, src, ACT.Copy).then_inc(wo_hi_ready, 1)

        def split_out_lo(dve, n):
            dve.wait_ge(raw_loaded[n % 2], raw_count(N_TILES + n, n % 2))
            dve.wait_ge(wo_hi_ready, n + 1)
            dst, src = out_part(wo_lo, n)
            hi, _ = out_part(wo_hi, n)
            nc.vector.tensor_tensor(dst, src, hi.bitcast(F32), ALU.subtract).then_inc(wo_lo_ready, 1)

        def m_cols(c):
            return slice(META + HALF * c, META + HALF * c + HALF)

        def split_m_hi(act, j, c):
            act.wait_ge(merged_step, 16 * (N_BRANCH - 1) + 2 * j + c + 1)
            act.wait_ge(groups_done, H_LAST_GROUP)
            nc.scalar.activation(h_hi[:, j, m_cols(c)], merged[:, j, HALF * c:HALF * c + HALF], ACT.Copy)\
                .then_inc(m_hi_ready, 1)

        def split_m_lo(dve, j, c):
            dve.wait_ge(m_hi_ready, KC * c + j + 1)
            nc.vector.tensor_tensor(h_lo[:, j, m_cols(c)], merged[:, j, HALF * c:HALF * c + HALF],
                                    h_hi[:, j, m_cols(c)].bitcast(F32), ALU.subtract).then_inc(m_lo_ready, 1)

        def out_bank(t, h):
            return (4 + 2 * t + h) % 8

        def out_count(t, h):
            return SIDE * h + t + 1 if t < SIDE else 2 * t + h + 1

        V_BANKS = (5, 6, 7, 2)
        STAT_BATCHES = (slice(0, 2), slice(2, 4), slice(4, 8), slice(8, 9))

        @block.scalar
        def _(act):
            s = nc.scalar

            def root(n):
                act.wait_ge(var_ready, n + 1)
                cols = STAT_BATCHES[n]
                s.activation(small[:, 0, cols], mv[:, cols, 1], ACT.Sqrt).then_inc(root_ready, 1)

            def normalise(c):
                part = xmeta if c == META_COL else xin[:, c, :]
                rows = META if c == META_COL else P
                s.activation(part, part, ACT.Identity, bias=nmr[0:rows, c:c + 1], scale=rstd[0:rows, c:c + 1])\
                    .then_inc(z_by_act, 1)

            def h_block(n):
                if n < 2 * KC and n not in HF_ON_DVE:
                    act.wait_ge(z_turned, n + 1)
                    if n >= 4:
                        wait_lo(act, n - 4)
                    s.activation(hf[:, n % 4, :], PS[:, 3 + n % 4, :], ACT.Identity,
                                 bias=column(ROW_B0 + n % KC), scale=column(ROW_G0 + n % KC))\
                        .then_inc(hf_by_act, 1)
                m = n - 1
                if n % KC:
                    h_hi_block(m)

            def h_hi_block(m):
                wait_hf(act, m)
                s.activation(h_hi[:, m % KC, block_cols(m)], hf[:, m % 4, :], ACT.Copy).then_inc(h_hi_ready, 1)

            root(0)
            act.wait_ge(rstd_ready, 1)
            normalise(0)
            normalise(1)
            split_hi(act, 0, 0, None)
            root(1)
            act.wait_ge(rstd_ready, 2)
            normalise(2)
            act.wait_ge(params_ready, 1)
            for n in range(KC):
                h_block(n)
                if n == 4:
                    root(2)
            h_hi_block(KC - 1)
            act.wait_ge(rstd_ready, 3)
            normalise(7)
            split_hi(act, 1, 1, None)
            for n in range(KC, 2 * KC):
                h_block(n)
            h_hi_block(2 * KC - 1)

            def read_group(sec, turn, g, dst, func=ACT.Copy, src_cols=None, last=True, **kw):
                b = sec.banks[g]
                a, z = src_cols
                act.wait_ge(groups_done, sec.groups(turn, g) + 1)
                ins = s.activation(dst, PS[:, b, a:z], func, **kw)
                if last:
                    ins.then_inc(bank_read[b], 1)

            wait_h_half(act, 1)
            for i in range(2):
                if i == 1:
                    split_hi(act, Q.tile(1, 1), 1, Q.groups(1, 0))
                for g in range(4):
                    n, c = g % 2, g // 2
                    if g == 3:
                        split_hi(act, Q.tile(i, 2), 0, Q.groups(i, 3))
                    read_group(Q, i, g, q_o[:, 2 * i + n, HALF * c:HALF * c + HALF], src_cols=(0, HALF))
                    if i == 0 and g == 1:
                        root(3)
                        act.wait_ge(rstd_ready, 4)
                        normalise(META_COL)
                if i == 0:
                    act.wait_ge(hfm_ready, 1)
                    s.activation(h_hi[:, :, 0:META], hfm, ACT.Copy).then_inc(h_hi_ready, 1)

            def stage_qk(i, n):
                chunk = i * 4 + n
                wait(act, scores_done, chunk)
                s.activation(q_stage[:], q_o[:, :, bass.ds(chunk * CHUNK, CHUNK)], ACT.Copy)\
                    .then_inc(qk_staged, 1)
                for g in range(2):
                    rows = slice(64 * g, 64 * g + 64)
                    s.activation(k_stage[rows, WIN_COLS[g]], kT[rows, bass.ds(chunk * CHUNK + META, 2 * CHUNK)],
                                 ACT.Copy).then_inc(qk_staged, 1)

            def stage_v(i, n):
                chunk = i * 4 + n
                wait(act, o_done, chunk)
                s.activation(v_stage[:, 0:3:2, :],
                             v_win[:, bass.ds(chunk, 1), :].rearrange("p w (g d) -> p (w g) d", g=2),
                             ACT.Copy).then_inc(v_staged, 1)

            def softmax_exp(i, n):
                chunk = i * 4 + n
                act.wait_ge(neg_m_ready, chunk + 1)
                wait(act, probs_turned, chunk)
                for c in range(2):
                    for g in range(2):
                        j, cols = 2 * c + g, slice(KEYS * g, KEYS * g + KEYS)
                        s.activation(probs[:, c, cols], S_PS[:, c, cols], ACT.Exp,
                                     bias=neg_m[:, j:j + 1], scale=SCALE, accum_out=row_sum[:, j:j + 1])\
                            .then_inc(probs_ready, 1)
                act.wait_ge(sink_m_ready, chunk + 1)
                s.activation(sink_e, sink_m, ACT.Exp).then_inc(sink_e_ready, 1)

            def copy_pT_meta(i, n):
                chunk = i * 4 + n
                act.wait_ge(probs_turned, chunk + 1)
                wait(act, o_done, chunk)
                s.activation(pT_meta[:], PTM_PS, ACT.Copy).then_inc(pT_meta_ready, 1)

            act.wait_ge(zeroed, N_ZEROED)
            for n, dst in enumerate((kT, vT)):
                split_next(act, split_hi, KV, 0, n, 3 * n)
                for c, (a, b) in enumerate(WITH_META):
                    parts = kv_parts(a, b)
                    for m, (p0, p1, col) in enumerate(parts):
                        read_group(KV, 0, 3 * n + c, dst[:, col:col + p1 - p0], src_cols=(p0, p1),
                                   last=m == len(parts) - 1)
                    if c == 0:
                        for b in range(3) if n else (0,):
                            act.wait_ge(bank_read[b], KV.used_end[b] - 1 + (n and b == 0))
                        for g in range(2):
                            rows, cols = slice(64 * g, 64 * g + 64), slice(META * g, META * g + META)
                            to = k_stage[rows, META_COLS][:, cols] if n == 0 else vT_meta_bd[rows, cols]
                            s.activation(to, dst[rows, 0:META], ACT.Copy).then_inc(meta_staged, 1)
                        if n == 1:
                            stage_qk(0, 0)

            def mix_turn(i, first=False):
                if not first:
                    stage_qk(i, 0)
                split_next(act, split_hi, MIX, i, 0, 0)
                softmax_exp(i, 0)
                stage_qk(i, 1)
                for g in range(11):
                    tile, c = min(g // 3, 3), g - 3 * min(g // 3, 3)
                    if c == 0 and tile > 0:
                        split_next(act, split_hi, MIX, i, tile, g)
                    if tile < 2:
                        a, b = WITH_META[c]
                        act.wait_ge(groups_done, MIX.groups(i, g) + 1)
                        if tile == 0:
                            wait(act, pooled_ready, i)
                        else:
                            wait(act, conv_ready, i)
                        read_group(MIX, i, g, (cu_sb, ac_sb)[tile][:, a:b], src_cols=(0, b - a))
                    if g in TURN_AFTER:
                        if first and g == TURN_AFTER[0]:
                            act.wait_ge(v_win_ready, 4)
                        stage_v(i, TURN_AFTER.index(g))
                        copy_pT_meta(i, TURN_AFTER.index(g))
                    if g in SCORES_AFTER:
                        n = SCORES_AFTER.index(g)
                        softmax_exp(i, n)
                        if n < 3:
                            stage_qk(i, n + 1)

            mix_turn(0, first=True)
            with act.Fori(1, 4) as i:
                mix_turn(i)

            for b in range(N_BRANCH):
                def z_turn(i):
                    for n in range(2):
                        split_next(act, split_hi, Z[b], i, n, 2 * n)
                        k = i * 2 + n
                        for c in range(2):
                            g = 2 * n + c
                            act.wait_ge(groups_done, Z[b].groups(i, g) + 1)
                            wait(act, y_f_ready, k * 2 + (8 * b + c - 1))
                            read_group(Z[b], i, g, silu[:, c, :], ACT.Silu, src_cols=(0, HALF))
                        for c in range(2):
                            act.wait_ge(y_f_ready, k * 2 + (8 * b + c + 1))
                            s.activation(y_hi[:, bass.ds(k, 1), HALF * c:HALF * c + HALF],
                                         y_f[:, bass.ds(c, 1), :], ACT.Copy).then_inc(y_hi_ready, 1)
                two_turns(act, z_turn, apart=b == 0)

                def gate_turn(i):
                    wait(act, merged_step, i * 8 + 16 * b)
                    s.activation(gate_bias[:], params[:, bass.ds(i * 4 + (ROW_BG + 8 * b), 4)], ACT.Copy)\
                        .then_inc(gate_bias_ready, 1)
                    act.wait_ge(gate_bias_ready, i + (2 * b + 1))
                    for pair in range(2):
                        last_pair = b == N_BRANCH - 1 and isinstance(i, int) and i == 1 and pair == 1
                        for n in range(2):
                            tile, g = 3 * pair + n, 8 * pair + 2 * n
                            split_next(act, split_hi, GATE[b], i, tile, g)
                            if last_pair and n == 1:
                                for piece in range(2):
                                    split_out_hi(act, piece)
                            for c in range(2):
                                act.wait_ge(groups_done, GATE[b].groups(i, g + c) + 1)
                                wait(act, merged_step, i * 8 + (16 * b + 4 * pair))
                                s.activation(sig[:, n, HALF * c:HALF * c + HALF], PS[:, GATE[b].banks[g + c], :],
                                             ACT.Sigmoid,
                                             bias=gate_bias[:, 2 * pair + n:2 * pair + n + 1])\
                                    .then_inc(bank_read[GATE[b].banks[g + c]], 1)
                        if not last_pair:
                            split_next(act, split_hi, GATE[b], i, 3 * pair + 2, 8 * pair + 4)

                two_turns(act, gate_turn, apart=b != 1)

            for piece in range(2, 4):
                split_out_hi(act, piece)
            for j in range(KC):
                split_m_hi(act, j, 0)
            act.wait_ge(groups_done, GROUPS_IN)
            for piece in range(4, OUT_PIECES):
                split_out_hi(act, piece)
            for j in range(KC):
                split_m_hi(act, j, 1)

            for t in range(T_TILES):
                act.wait_ge(var2_ready, t + 1)
                s.activation(small2[:, 1, t:t + 1], small2[:, 0, t:t + 1], ACT.Sqrt).then_inc(root2_ready, 1)

        @block.vector
        def _(dve):
            v = nc.vector
            steps = [0]

            def then(ins):
                ins.then_inc(dve_step, 1)
                steps[0] += 1
                dve.wait_ge(dve_step, steps[0])

            def rsqrt(var, root, r, a):
                then(v.reciprocal(r, root))
                then(v.tensor_tensor(a, r, r, ALU.mult))
                then(v.tensor_tensor(a, a, var, ALU.mult))
                then(v.tensor_scalar(a, a, -0.5, 1.5, ALU.mult, ALU.add))
                then(v.tensor_tensor(r, r, a, ALU.mult))

            def row_stats(c):
                dve.wait_ge(x_loaded[c], 16)
                rows = META if c == META_COL else P
                part = xmeta if c == META_COL else xin[:, c, :]
                v.bn_stats(stats[0:rows, c, 0, :], part[:, 0:HALF]).then_inc(dve_step, 1)
                v.bn_stats(stats[0:rows, c, 1, :], part[:, HALF:D]).then_inc(dve_step, 1)
                steps[0] += 2
                dve.wait_ge(dve_step, steps[0])
                then(v.bn_aggr(mv[0:rows, c, :], stats[0:rows, c, :, :]))

            def row_rstd(n, meanwhile=None):
                cols = STAT_BATCHES[n]
                v.tensor_scalar(mv[:, cols, 1], mv[:, cols, 1], LN_EPS, None, ALU.add).then_inc(var_ready, 1)
                if meanwhile:
                    meanwhile()
                dve.wait_ge(root_ready, n + 1)
                rsqrt(mv[:, cols, 1], small[:, 0, cols], rstd[:, cols], small[:, 1, cols])
                v.scalar_tensor_tensor(nmr[:, cols], mv[:, cols, 0], -1.0, rstd[:, cols], ALU.mult, ALU.mult)\
                    .then_inc(rstd_ready, 1)

            def normalise(c):
                v.tensor_scalar(xin[:, c, :], xin[:, c, :], rstd[:, c:c + 1], nmr[:, c:c + 1],
                                ALU.mult, ALU.add).then_inc(z_by_dve, 1)

            def copy_params():
                dve.wait_ge(params_turned, 1)
                v.tensor_copy(params[:], PS[:, 7, 0:N_ROWS]).then_inc(params_ready, 1)

            def lo_block(n):
                dve.wait_ge(h_hi_ready, n + 1)
                cols = block_cols(n)
                v.tensor_tensor(h_lo[:, n % KC, cols], hf[:, n % 4, :], h_hi[:, n % KC, cols].bitcast(F32),
                                ALU.subtract).then_inc(h_lo_by_dve, 1)

            dve.wait_ge(zeroed, 1)
            row_stats(0)
            row_stats(1)
            row_rstd(0)
            row_stats(2)
            row_stats(3)
            row_rstd(1, meanwhile=copy_params)
            dve.wait_ge(rstd_ready, 2)
            normalise(3)
            for c in range(4, 8):
                row_stats(c)

            def lo_parts():
                split_lo(dve, 0, 0, None)
                lo_block(3)

            row_rstd(2, meanwhile=lo_parts)
            dve.wait_ge(rstd_ready, 3)
            normalise(4)
            normalise(5)
            lo_block(7)
            normalise(6)
            split_lo(dve, 1, 1, None)
            dve.wait_ge(params_ready, 1)
            for n in HF_ON_DVE:
                dve.wait_ge(z_turned, n + 1)
                wait_lo(dve, n - 4)
                v.tensor_scalar(hf[:, n % 4, :], PS[:, 3 + n % 4, :], column(ROW_G0 + n % KC),
                                column(ROW_B0 + n % KC), ALU.mult, ALU.add).then_inc(hf_by_dve, 1)
                lo_block(n)
            row_stats(META_COL)
            row_rstd(3)
            dve.wait_ge(rows0_loaded, 32)
            for row in (gain0, bias0):
                v.tensor_scalar(row, row, ALPHA, None, ALU.mult).then_inc(rows0_scaled, 1)
            dve.wait_ge(z_turned, 2 * KC + 1)
            zm = PS[:, 7, P:2 * P].rearrange("p (k m) -> p k m", m=META)
            gain = params[:, ROW_G0:ROW_G0 + KC].unsqueeze(2).to_broadcast([P, KC, META])
            bias = params[:, ROW_B0:ROW_B0 + KC].unsqueeze(2).to_broadcast([P, KC, META])
            then(v.tensor_tensor(hfm, zm, gain, ALU.mult))
            v.tensor_tensor(hfm, hfm, bias, ALU.add).then_inc(hfm_ready, 1)

            dve.wait_ge(sinks_loaded, 16)
            for e in range(2):
                rows = slice(64 * e, 64 * e + 64)
                then(v.tensor_copy(sink[rows, :].rearrange("p (c g) -> p c g", c=2),
                                   all_sinks[rows, :].rearrange("p (g c e) -> p c g e", g=2, c=2)[:, :, :, e]))
            then(v.tensor_scalar(neg_sink[:], sink[:], -1.0, None, ALU.mult))

            split_lo(dve, Q.tile(0, 2), 0, Q.groups(0, 3))
            split_lo(dve, Q.tile(1, 1), 1, Q.groups(1, 0))
            split_lo(dve, Q.tile(1, 2), 0, Q.groups(1, 3))
            for n in range(2):
                split_next(dve, split_lo, KV, 0, n, 3 * n)

            def copy_v_windows():
                for n, bank in enumerate(V_BANKS):
                    dve.wait_ge(v_turned, n + 1)
                    v.tensor_copy(v_win[:, 4 * n:4 * n + 4, :],
                                  PS[:, bank, :].rearrange("p (w c) -> p w c", w=4)).then_inc(v_win_ready, 1)

            def softmax_max(i, n, first=False):
                chunk = i * 4 + n
                dve.wait_ge(scores_done, chunk + 1)
                if first:
                    for g in range(2):
                        before = slice(WIN_COLS[g].start, WIN_COLS[g].start + CHUNK)
                        then(v.memset(S_PS[:, :, before], NEG_INF / SCALE))
                then_loop(i, v.tensor_reduce(row_max.rearrange("p (c g) -> p c g", c=2),
                                             S_PS.rearrange("p c (g k) -> p c g k", g=2), AX_X, ALU.max))
                wait(dve, sink_e_ready, chunk)
                v.scalar_tensor_tensor(neg_m, row_max, -SCALE, neg_sink[:], ALU.mult, ALU.min)\
                    .then_inc(neg_m_ready, 1)
                dve.wait_ge(neg_m_ready, chunk + 1)
                v.tensor_tensor(sink_m, neg_m, sink[:], ALU.add).then_inc(sink_m_ready, 1)

            def then_loop(turn, ins):
                ins.then_inc(conv_step, 1)
                loop_steps[0] += 1
                dve.wait_ge(conv_step, turn * STEPS + loop_steps[0])

            def scale_probs(i, n):
                chunk = i * 4 + n
                dve.wait_ge(probs_ready, chunk * 4 + 4)
                dve.wait_ge(sink_e_ready, chunk + 1)
                then_loop(i, v.tensor_tensor(denom, row_sum, sink_e, ALU.add))
                then_loop(i, v.reciprocal(r_den, denom))
                p4 = probs[:].rearrange("p c (g k) -> p (c g) k", g=2)
                v.tensor_tensor(p4, p4, r_den.unsqueeze(2).to_broadcast([P, 4, KEYS]), ALU.mult)\
                    .then_inc(probs_scaled, 1)

            def copy_pT(i, n):
                chunk = i * 4 + n
                dve.wait_ge(probs_turned, chunk + 1)
                wait(dve, o_done, chunk)
                v.tensor_copy(pT[:], PT_PS).then_inc(pT_ready, 1)

            def copy_o(i, n):
                chunk = i * 4 + n
                dve.wait_ge(o_done, chunk + 1)
                v.tensor_copy(q_o[:, :, bass.ds(chunk * CHUNK, CHUNK)], O_PS).then_inc(o_ready, 1)

            STEPS = 4 * 3 + 2
            loop_steps = [0]

            def mix_turn(i, first=False):
                loop_steps[0] = 0
                softmax_max(i, 0, first)
                for g in range(11):
                    tile, c = min(g // 3, 3), g - 3 * min(g // 3, 3)
                    if g + 1 in TURN_AFTER:
                        scale_probs(i, TURN_AFTER.index(g + 1))
                    if c == 0:
                        split_next(dve, split_lo, MIX, i, tile, g)
                    if tile == 2:
                        a, b = WITH_META[c]
                        dve.wait_ge(bank_read[MIX.banks[3 + c]], MIX.used(i, 3 + c) + 1)
                        dve.wait_ge(groups_done, MIX.groups(i, g) + 1)
                        v.tensor_tensor(u_sb[:, a:b], PS[:, MIX.banks[g], 0:b - a], ac_sb[:, a:b], ALU.mult)\
                            .then_inc(bank_read[MIX.banks[g]], 1)
                        if c == 2:
                            for j in range(3):
                                dve.wait_ge(bank_read[MIX.banks[6 + j]], MIX.used(i, 6 + j) + 1)
                            if first:
                                dve.wait_ge(skip_stored, 16 * T_TILES)
                            dst = conv_out[:, bass.ds(i, 1), :]
                            u3 = u_sb[:].unsqueeze(1)
                            tap = [params[:, bass.ds(i + (ROW_CONV + 4 * j), 1)] for j in range(3)]
                            then_loop(i, v.tensor_scalar(dst, u3[:, :, META:TOK], tap[2], None, ALU.mult))
                            for back in (1, 2):
                                ins = v.scalar_tensor_tensor(dst, u3[:, :, META - back:TOK - back],
                                                             tap[2 - back], dst, ALU.mult, ALU.add)
                                if back == 1:
                                    then_loop(i, ins)
                                else:
                                    ins.then_inc(conv_ready, 1)
                    if tile == 3:
                        dve.wait_ge(groups_done, MIX.groups(i, g) + 1)
                        dve.wait_ge(conv_ready, i + 1)
                        dst = conv_out[:, bass.ds(i, 1), HALF * c:HALF * c + HALF]
                        v.tensor_tensor(dst, PS[:, MIX.banks[g]:MIX.banks[g] + 1, :], dst, ALU.mult)\
                            .then_inc(bank_read[MIX.banks[g]], 1)
                    if g in TIMES_V_AFTER:
                        copy_o(i, TIMES_V_AFTER.index(g))
                    if g in TURN_AFTER:
                        copy_pT(i, TURN_AFTER.index(g))
                    if first and g == 0:
                        copy_v_windows()
                    if first and g == 1:
                        dve.wait_ge(v_turned, 5)
                        v.tensor_copy(v_meta_bd[:], PS[0:2 * META, 7, 0:P]).then_inc(v_meta_ready, 1)
                    if g in SCORES_AFTER:
                        softmax_max(i, SCORES_AFTER.index(g))
                assert loop_steps[0] == STEPS, loop_steps

            mix_turn(0, first=True)
            with dve.Fori(1, 4) as i:
                mix_turn(i)

            for n in range(8):
                i, c = n // 2, n % 2
                dve.wait_ge(groups_done, MAP.groups(0, n) + 1)
                v.tensor_scalar(pooled[:, i, HALF * c:HALF * c + HALF], PS[:, MAP.banks[n], :],
                                column(ROW_PS + i), None, ALU.mult).then_inc(bank_read[MAP.banks[n]], 1)

            for b in range(4):
                dve.wait_ge(bank_read[b], MAP.used_end[b])
            dve.wait_ge(o_ready, N_CHUNKS)
            for b, mixed in enumerate((conv_out, q_o, pooled)):
                def z_turn(i):
                    for n in range(2):
                        split_next(dve, split_lo, Z[b], i, n, 2 * n)
                        k = i * 2 + n
                        for c in range(2):
                            g = 2 * n + c
                            dve.wait_ge(bank_read[Z[b].banks[g]], Z[b].used(i, g) + 1)
                            wait(dve, y_hi_ready, k * 2 + (8 * b))
                            wait(dve, y_lo_ready, k * 2 + (8 * b))
                            v.tensor_tensor(y_f[:, bass.ds(c, 1), :], silu[:, bass.ds(c, 1), :],
                                            mixed[:, bass.ds(k, 1), HALF * c:HALF * c + HALF], ALU.mult)\
                                .then_inc(y_f_ready, 1)
                        for c in range(2):
                            dve.wait_ge(y_f_ready, k * 2 + (8 * b + c + 1))
                            dve.wait_ge(y_hi_ready, k * 2 + (8 * b + c + 1))
                            cols = slice(HALF * c, HALF * c + HALF)
                            v.tensor_tensor(y_lo[:, bass.ds(k, 1), cols], y_f[:, bass.ds(c, 1), :],
                                            y_hi[:, bass.ds(k, 1), cols].bitcast(F32), ALU.subtract)\
                                .then_inc(y_lo_ready, 1)
                def gate_turn(i):
                    for pair in range(2):
                        last_pair = b == N_BRANCH - 1 and isinstance(i, int) and i == 1 and pair == 1
                        for n in range(2):
                            split_next(dve, split_lo, GATE[b], i, 3 * pair + n, 8 * pair + 2 * n)
                        if last_pair:
                            for piece in range(4):
                                split_out_lo(dve, piece)
                            for j in range(KC - 2):
                                split_m_lo(dve, j, 0)
                        else:
                            split_next(dve, split_lo, GATE[b], i, 3 * pair + 2, 8 * pair + 4)
                        for n in range(2):
                            for c in range(2):
                                g, gate = 8 * pair + 4 + 2 * n + c, 8 * pair + 2 * n + c
                                bank, cols = GATE[b].banks[g], slice(HALF * c, HALF * c + HALF)
                                out_at = merged[:, bass.ds(i * 4 + (2 * pair + n), 1), cols]
                                prod = sig[:, n:n + 1, cols]
                                dve.wait_ge(groups_done, GATE[b].groups(i, g) + 1)
                                dve.wait_ge(bank_read[GATE[b].banks[gate]], GATE[b].used(i, gate) + 1)
                                v.tensor_tensor(prod, PS[:, bank:bank + 1, :], prod, ALU.mult)\
                                    .then_inc(bank_read[bank], 1)
                                dve.wait_ge(bank_read[bank], GATE[b].used(i, g) + 1)
                                if b == 0:
                                    v.tensor_copy(out_at, prod).then_inc(merged_step, 1)
                                else:
                                    v.tensor_tensor(out_at, out_at, prod, ALU.add).then_inc(merged_step, 1)
                                if last_pair and c == 0:
                                    split_m_lo(dve, KC - 2 + n, 0)

                two_turns(dve, z_turn, apart=b == 0)
                wait(dve, merged_step, 16 * b)
                two_turns(dve, gate_turn, apart=b != 1)

            for piece in range(4, OUT_PIECES):
                split_out_lo(dve, piece)
            for j in range(KC):
                split_m_lo(dve, j, 1)

            dve.wait_ge(rows1_loaded, 32)
            for t in range(T_TILES):
                dve.wait_ge(skip_loaded[t % SKIP_SLOTS], 16 * (t // SKIP_SLOTS + 1))
                if t >= 2:
                    dve.wait_ge(stored[t % 2], 16 * (t // 2))
                for h in range(2):
                    dve.wait_ge(out_done, out_count(t, h))
                    cols = slice(HALF * h, HALF * h + HALF)
                    v.tensor_tensor(res[:, t % 2, cols], PS[:, out_bank(t, h), :],
                                    skip[:, t % SKIP_SLOTS, cols], ALU.add).then_inc(res_half, 1)
                    dve.wait_ge(res_half, 2 * t + h + 1)
                    then(v.bn_stats(stats2[:, t, h, :], res[:, t % 2, cols]))
                then(v.bn_aggr(mv2[:, t, :], stats2[:, t, :, :]))
                var, root, r, a = (small2[:, n, t:t + 1] for n in range(4))
                v.tensor_scalar(var, mv2[:, t, 1:2], LN_EPS, None, ALU.add).then_inc(var2_ready, 1)
                then(v.scalar_tensor_tensor(res[:, t % 2, :], res[:, t % 2, :], mv2[:, t, 0:1], gain1,
                                            ALU.subtract, ALU.mult))
                dve.wait_ge(var2_ready, t + 1)
                dve.wait_ge(root2_ready, t + 1)
                rsqrt(var, root, r, a)
                for part in ((0, D),) if t < T_TILES - 1 else ((0, HALF), (HALF, D)):
                    rows = res[:, t % 2, slice(*part)]
                    v.scalar_tensor_tensor(rows, rows, r, bias1[:, slice(*part)], ALU.mult, ALU.add)\
                        .then_inc(row_ready, 1)

        @block.tensor
        def _(pe):
            mm = nc.tensor.matmul
            turn = nc.tensor.transpose

            pe.wait_ge(ident_ready, 2)
            pe.wait_ge(params_loaded, 16 * 5)
            turn(PS[:, 7, 0:N_ROWS], prow, ident[0:N_ROWS, 0:N_ROWS]).then_inc(params_turned, 1)
            def turn_z(blocks):
                for n in blocks:
                    half, k = n // KC, n % KC
                    pe.wait_ge(z_by_act, (3, 4)[half])
                    pe.wait_ge(z_by_dve, (1, 4)[half])
                    if n >= 4:
                        wait_hf(pe, n - 4)
                    for t in range(4):
                        last = turn(PS[:, 3 + n % 4, P * t:P * t + P], xin[:, 4 * half + t, P * k:P * k + P],
                                    ident[:])
                    last.then_inc(z_turned, 1)

            def turn_z_meta():
                pe.wait_ge(z_by_act, 5)
                pe.wait_ge(params_ready, 1)
                for k in range(KC):
                    last = turn(PS[:, 7, P + META * k:P + META * k + META], xmeta[:, P * k:P * k + P],
                                ident[0:META, 0:META])
                last.then_inc(z_turned, 1)

            def three_passes(dst, w_parts, x_parts, n_k, begin=True, end=True, after_first=None):
                (wh, wl), (xh, xl) = w_parts, x_parts
                for k in range(n_k):
                    if after_first and k == 1:
                        after_first()
                    for p, (a, b) in enumerate(((wh, xh), (wh, xl), (wl, xh))):
                        last = mm(dst, a(k), b(k), start=begin and k == 0 and p == 0,
                                  stop=end and k == n_k - 1 and p == 2)
                return last

            def project(sec, i, g, slot, tokens, more=0, after_first=None):
                b = sec.banks[g]
                a, z = tokens
                wait(pe, bank_read[b], sec.used(i, g) + more)
                three_passes(PS[:, b, 0:z - a],
                             (lambda k: w_hi[:, slot, k, :], lambda k: w_lo[:, slot, k, :]),
                             (lambda k: h_hi[:, k, a:z], lambda k: h_lo[:, k, a:z]), KC, after_first=after_first)\
                    .then_inc(groups_done, 1)

            turn_z(range(KC))
            for _ in range(24):
                mm(PS[:, 2, 0:P], ident[:], ident[:], start=True, stop=True)
            for i in range(2):
                for g in range(4):
                    n, c = g % 2, g // 2
                    if c == 0:
                        pe.wait_ge(w_lo_ready, Q.tile(i, n) + 1)
                    if i == 0 and n == 0:
                        wait_h_half(pe, c)
                    turn_next = None
                    if i == 0 and c == 0:
                        turn_next = lambda: turn_z(range(KC + 4 * n, KC + 4 * n + 4))
                    project(Q, i, g, n, REAL_ONLY[c], after_first=turn_next)
                    if i == 0 and g == 2:
                        turn_z_meta()
            pe.wait_ge(meta_lo_ready, 1)
            for n in range(2):
                pe.wait_ge(w_lo_ready, KV.tile(0, n) + 1)
                for c in range(3):
                    project(KV, 0, 3 * n + c, n, WITH_META[c])

            def turn_v_windows():
                for b in range(3):
                    pe.wait_ge(bank_read[b], KV.used_end[b])
                for c in range(N_CHUNKS):
                    last = turn(PS[:, V_BANKS[c // 4], P * (c % 4):P * (c % 4) + P],
                                vT[:, META + CHUNK * c:META + CHUNK * c + P], ident[:])
                    if c % 4 == 3:
                        last.then_inc(v_turned, 1)

            def turn_v_meta():
                turn(PS[0:2 * META, 7, 0:P], vT_meta_bd[:], ident[:]).then_inc(v_turned, 1)

            pe.wait_ge(zeroed, N_ZEROED)
            pe.wait_ge(meta_staged, 4)

            def scores(i, n):
                chunk = i * 4 + n
                pe.wait_ge(qk_staged, chunk * 3 + 3)
                wait(pe, probs_ready, chunk * 4)
                for c in range(2):
                    last = mm(S_PS[:, c, :], q_stage[:, 2 * c:2 * c + 2, :].rearrange("p t q -> p (t q)"),
                              k_stage[:], start=True, stop=True)
                last.then_inc(scores_done, 1)

            def turn_probs(i, n):
                chunk = i * 4 + n
                pe.wait_ge(probs_scaled, chunk + 1)
                wait(pe, pT_ready, chunk)
                wait(pe, pT_meta_ready, chunk)
                for c in range(2):
                    for g in range(2):
                        turn(PT_PS[:, g, c, :], probs[:, c, WIN_COLS[g]], ident[:])
                    last = turn(PTM_PS[:, c, :], probs[:, c, META_COLS], ident[:])
                last.then_inc(probs_turned, 1)

            def times_v(i, n):
                chunk = i * 4 + n
                pe.wait_ge(v_staged, chunk + 1)
                pe.wait_ge(pT_ready, chunk + 1)
                pe.wait_ge(pT_meta_ready, chunk + 1)
                wait(pe, o_ready, chunk)
                out_at = PS[:, 7, 0:4 * CHUNK]
                mm(out_at, v_meta_bd[:], pT_meta[:].rearrange("p c r -> p (c r)"), start=True, stop=False)
                for g in range(2):
                    last = mm(out_at, v_stage[:, g:g + 2, :].rearrange("p z d -> p (z d)"),
                              pT[:, g, :, :].rearrange("p c r -> p (c r)"), start=False, stop=g == 1)
                last.then_inc(o_done, 1)

            def mix_turn(i, first=False):
                scores(i, 0)
                for g in range(11):
                    tile, c = min(g // 3, 3), g - 3 * min(g // 3, 3)
                    if c == 0:
                        pe.wait_ge(w_lo_ready, MIX.tile(i, tile) + 1)
                    project(MIX, i, g, tile % 2, (WITH_META if tile < 3 else REAL_ONLY)[c],
                            after_first=turn_v_meta if first and g == 2 else None)
                    if first and g == 0:
                        turn_v_windows()
                    if g in TIMES_V_AFTER:
                        if first and g == TIMES_V_AFTER[0]:
                            pe.wait_ge(v_meta_ready, 1)
                        times_v(i, TIMES_V_AFTER.index(g))
                    if g in TURN_AFTER:
                        if first and g == TURN_AFTER[0]:
                            pe.wait_ge(v_win_ready, 4)
                        turn_probs(i, TURN_AFTER.index(g))
                    if g in SCORES_AFTER:
                        scores(i, SCORES_AFTER.index(g))

            mix_turn(0, first=True)
            with pe.Fori(1, 4) as i:
                mix_turn(i)

            pe.wait_ge(pool_w_loaded, 16)
            pe.wait_ge(pooled_ready, 4)
            pe.wait_ge(probs_ready, 4 * N_CHUNKS)
            for n in range(8):
                g, c = n // 2, n % 2
                pe.wait_ge(bank_read[MAP.banks[n]], MAP.used(0, n))
                mm(PS[:, MAP.banks[n], :], pool_wt[:, g, :], pooled[:, g, HALF * c:HALF * c + HALF],
                   start=True, stop=True).then_inc(groups_done, 1)

            with pe.Fori(0, N_BRANCH) as b:
                with pe.Fori(0, 2) as i:
                    for n in range(2):
                        pe.wait_ge(w_lo_ready, b * BRANCH_TILES + Z[0].tile(i, n) + 1)
                        for c in range(2):
                            project(Z[0], i, 2 * n + c, n, REAL_ONLY[c], more=b * BRANCH_USES)
                with pe.Fori(0, 2) as i:
                    for pair in range(2):
                        for n in range(2):
                            tile = 3 * pair + n
                            pe.wait_ge(w_lo_ready, b * BRANCH_TILES + GATE[0].tile(i, tile) + 1)
                            for c in range(2):
                                project(GATE[0], i, 8 * pair + 2 * n + c, tile % 2, REAL_ONLY[c],
                                        more=b * BRANCH_USES)
                        tile = 3 * pair + 2
                        pe.wait_ge(w_lo_ready, b * BRANCH_TILES + GATE[0].tile(i, tile) + 1)
                        pe.wait_ge(y_lo_ready, b * 8 + 8)
                        wh, wl = (w[:, tile % 2, :, :].rearrange("p (k two) c -> p k (two c)", two=2)
                                  for w in (w_hi, w_lo))
                        for n in range(2):
                            for c in range(2):
                                g = 8 * pair + 4 + 2 * n + c
                                bank = GATE[0].banks[g]
                                pe.wait_ge(bank_read[bank], GATE[0].used(i, g) + b * BRANCH_USES)
                                three_passes(PS[:, bank, :],
                                             (lambda k: wh[:, k, P * n:P * n + P],
                                              lambda k: wl[:, k, P * n:P * n + P]),
                                             (lambda k: y_hi[:, k, HALF * c:HALF * c + HALF],
                                              lambda k: y_lo[:, k, HALF * c:HALF * c + HALF]), 4)\
                                    .then_inc(groups_done, 1)

            def out_rows_product(t, h, k0, k1):
                tokens = slice(META + P * t, META + P * t + P)
                return three_passes(PS[:, out_bank(t, h), :],
                                    (lambda k: h_hi[:, k0 + k, tokens], lambda k: h_lo[:, k0 + k, tokens]),
                                    (lambda k: wo_hi[h][:, k0 + k, :], lambda k: wo_lo[h][:, k0 + k, :]),
                                    k1 - k0, begin=k0 == 0, end=k1 == KC)

            for n in range(OUT_PIECES):
                h, k = n // 4, 2 * (n % 4)
                pe.wait_ge(wo_lo_ready, n + 1)
                if h == 0:
                    pe.wait_ge(m_lo_ready, k + 2)
                for t in range(SIDE):
                    last = out_rows_product(t, h, k, k + 2)
                    if k == KC - 2:
                        last.then_inc(out_done, 1)
            for t in range(SIDE, T_TILES):
                if t == 4:
                    pe.wait_ge(m_lo_ready, 2 * KC)
                for h in range(2):
                    bank = out_bank(t, h)
                    if t < 4:
                        pe.wait_ge(bank_read[bank], GATE[-1].used_end[bank])
                    else:
                        pe.wait_ge(res_half, 2 * (t - 4) + h + 1)
                    out_rows_product(t, h, 0, KC).then_inc(out_done, 1)


_INS = ['x', 'meta_tokens', 'ln0_g', 'ln0_b', 'w_in', 'b_gate', 'conv_w', 'attn_sinks', 'pool_w', 'pool_scale',
        'w_br_a', 'w_br_b', 'w_br_c', 'w_out', 'ln_g', 'ln_b']
_OUTS = [((1, 1024, 1024), 'float32')]


def kernel(**inputs):
    import numpy as _np
    import concourse.bacc as _bacc
    from concourse import mybir as _mybir
    from concourse.bass_utils import run_bass_kernel_spmd as _run

    nc = _bacc.Bacc("TRN2", target_bir_lowering=False, num_devices=1)
    arrays, args = {}, []
    for name in _INS:
        a = _np.ascontiguousarray(inputs[name])
        arrays[f"in_{name}_dram"] = a
        args.append(nc.dram_tensor(f"in_{name}_dram", a.shape, _mybir.dt.from_np(a.dtype), kind="ExternalInput").ap())
    for i, (shape, dtype) in enumerate(_OUTS):
        dt = _mybir.dt.from_np(_np.dtype(dtype))
        args.append(nc.dram_tensor(f"out_{i}_dram", shape, dt, kind="ExternalOutput").ap())
    hybrid_layer(nc, *args)
    r = _run(nc, [arrays], core_ids=[0])
    return r.results[0]["out_0_dram"]
```

```python
from contextlib import ExitStack

import concourse.bass as bass
from concourse import mybir

F32 = mybir.dt.float32
F32R = mybir.dt.float32r
ALU = mybir.AluOpType
ACT = mybir.ActivationFunctionType
AX_X = mybir.AxisListType.X

P = 128
D = 1024
KC = D // P
SEQ = 1024
META = 16
TOK = META + SEQ
CHUNK = 64
N_CHUNKS = SEQ // CHUNK
HEAD = 64
PAD = CHUNK
KEYS = META + 2 * CHUNK
LN_EPS = 1e-5
NEG_INF = -1e30
ALPHA = 2 ** 0.25
SCALE = HEAD ** -0.5
POOL_WINDOWS = (2, 4, 8, 16)
N_BRANCH = 3
CONV_K = 3
HALF = 512

COL_AB, COL_AC, COL_AH, COL_AZ = 0, 512, 1024, 1536
COL_Q, COL_K, COL_V, COL_BZ = 2048, 2560, 2688, 2816
COL_CU, COL_CZ, COL_GATE = 3328, 3840, 4352

WITH_META = ((0, 348), (348, 694), (694, TOK))
CONV_START = META - (CONV_K - 1)
FOR_CONV = tuple((CONV_START + (TOK - CONV_START) * c // 3, CONV_START + (TOK - CONV_START) * (c + 1) // 3)
                 for c in range(3))
REAL_ONLY = ((META, META + HALF), (META + HALF, TOK))

SCORES_AFTER = (0, 2, 5, 7)
TURN_AFTER = (2, 4, 7, 9)
TIMES_V_AFTER = (3, 5, 8, 10)
PASSES = ((0, 0), (0, 1), (1, 0))
N_ZEROED = 6

HF_ON_DVE = (5, 9, 11, 13, 15)
LO_ON_DVE = (7, 9, 11, 13, 15)

ROW_G0, ROW_B0, ROW_BG, ROW_CONV, ROW_PS = 0, 8, 16, 40, 52
N_ROWS = 56


class Section:

    def __init__(self, before, banks, tiles, turns):
        self.tile0 = before.tile_end if before else 0
        self.group0 = before.group_end if before else 0
        self.used0 = list(before.used_end) if before else [0] * 4
        self.banks, self.tiles, self.turns = banks, tiles, turns
        self.per_turn = [banks.count(b) for b in range(4)]
        self.tile_end = self.tile0 + tiles * turns
        self.group_end = self.group0 + len(banks) * turns
        self.used_end = [u + n * turns for u, n in zip(self.used0, self.per_turn)]

    def tile(self, turn, n):
        return turn * self.tiles + (self.tile0 + n)

    def groups(self, turn, g):
        return turn * len(self.banks) + (self.group0 + g)

    def used(self, turn, g):
        b = self.banks[g]
        return turn * self.per_turn[b] + (self.used0[b] + self.banks[:g].count(b))


def wait(eng, sem, value):
    if not isinstance(value, int) or value > 0:
        eng.wait_ge(sem, value)


def hybrid_layer(nc, x, meta_tokens, ln0_g, ln0_b, w_in, b_gate, conv_w, attn_sinks, pool_w, pool_scale,
                 w_br_a, w_br_b, w_br_c, w_out, ln_g, ln_b, out):
    Q = Section(None, (0, 1, 2, 1), 2, 2)
    KV = Section(Q, (0, 1, 2, 0, 1, 2), 2, 1)
    MIX = Section(KV, (0, 1, 2, 0, 1, 2, 0, 1, 2, 0, 1), 4, 4)
    MAP = Section(MIX, (0, 1, 2, 3, 0, 1, 2, 3), 0, 1)
    Z, GATE = [], []
    last = MAP
    for _ in range(N_BRANCH):
        Z.append(Section(last, (0, 1, 2, 3), 2, 2))
        GATE.append(Section(Z[-1], (0, 1, 2, 3) * 4, 6, 2))
        last = GATE[-1]
    N_TILES = last.tile_end
    GROUPS_IN = last.group_end
    BRANCH_TILES = GATE[0].tile_end - Z[0].tile0
    BRANCH_USES = GATE[0].used_end[0] - Z[0].used0[0]
    OUT_PIECES = 8
    H_LAST_GROUP = GROUPS_IN - 4
    T_TILES = SEQ // P
    SKIP_SLOTS = 4
    SKIP_ORDER = (4, 5, 6, 7, 0, 1, 2, 3)
    SIDE = 2

    with ExitStack() as ctx:
        def sb(name, shape, dt=F32, stack=ctx):
            return stack.enter_context(nc.sbuf_tensor(name, shape, dt))

        def sem(name):
            return ctx.enter_context(nc.semaphore(name))

        h_hi = sb("h_hi", [P, KC, TOK], F32R)
        h_lo = sb("h_lo", [P, KC, TOK], F32R)
        raw = sb("raw", [P, 2, KC, P])
        w_hi = sb("w_hi", [P, 2, KC, P], F32R)
        w_lo = sb("w_lo", [P, 2, KC, P], F32R)
        merged = sb("merged", [P, KC, SEQ])
        ident = sb("ident", [P, P])
        params = sb("params", [P, N_ROWS])
        rstd = sb("rstd", [P, 1 + T_TILES])
        nmr = sb("nmr", [P, 1 + T_TILES])
        gate_bias = sb("gate_bias", [P, 4])

        conv_out = merged[:, 0:4, :]
        xin = merged
        v_win = merged[:, 4:8, :].rearrange("p f (w c) -> p (f w) c", c=P)\
            .rearrange("p (h w) c -> p h w c", h=2).bitcast(F32R)

        def column(row):
            return params[:, row:row + 1]

        qm = ExitStack()
        q_o = sb("q_o", [P, 4, SEQ], stack=qm)
        pooled = sb("pooled", [P, 4, SEQ], stack=qm)
        hf = q_o[:, :, 0:HALF]
        gain0 = pooled[:, 3, :]
        xmeta = pooled[0:META, 0, :]
        META_COL = T_TILES
        prow = pooled[0:N_ROWS, 1, 0:P]
        hfm = pooled[:, 2, 0:P].rearrange("p (k m) -> p k m", m=META)

        one = ExitStack()
        kT = sb("kT", [P, 2, META + PAD + SEQ], F32R, stack=one)
        vT = sb("vT", [P, META + PAD + SEQ], stack=one)
        v_meta = sb("v_meta", [6 * META, P], F32R, stack=one)
        vT_meta_bd = sb("vT_meta_bd", [P, 2 * META], stack=one)
        q_stage = sb("q_stage", [P, 2, 4, CHUNK], F32R, stack=one)
        k_stage = sb("k_stage", [P, 2, 2 * KEYS], F32R, stack=one)
        v_stage = sb("v_stage", [P, 2, 3, HEAD], F32R, stack=one)
        probs = sb("probs", [P, 2, 2 * KEYS], stack=one)
        pT = sb("pT", [P, 2, 2, 2 * P], F32R, stack=one)
        pT_meta = sb("pT_meta", [6 * META, 2 * P], F32R, stack=one)
        ac_sb = sb("ac_sb", [P, TOK], stack=one)
        u_sb = sb("u_sb", [P, TOK], stack=one)
        cu_sb = sb("cu_sb", [P, TOK], stack=one)
        win_a = sb("win_a", [P, TOK], stack=one)
        win_b = sb("win_b", [P, TOK], stack=one)
        bias0 = win_a[:, 0:D]
        pool_wt = sb("pool_wt", [P, 4, P], stack=one)
        small = sb("small", [P, 8, 16], stack=one)
        stats = sb("stats", [P, 1 + T_TILES, 2, 6], stack=one)
        mv = sb("mv", [P, 1 + T_TILES, 2], stack=one)
        neg_sink = sb("neg_sink", [P, 4], stack=one)
        sink = sb("sink", [P, 4], stack=one)
        all_sinks = sb("all_sinks", [P, 8], stack=one)
        one.close()
        row_max, neg_m, sink_m, sink_e = (small[:, n, 0:4] for n in range(4))
        row_sum, denom, r_den = (small[:, n, 0:4] for n in range(4, 7))

        two = ExitStack()
        y_hi = sb("y_hi", [P, 4, SEQ], F32R, stack=two)
        y_lo = sb("y_lo", [P, 4, SEQ], F32R, stack=two)
        silu = sb("silu", [P, 2, HALF], stack=two)
        y_f = sb("y_f", [P, 2, HALF], stack=two)
        sig = sb("sig", [P, 2, SEQ], stack=two)
        two.close()
        qm.close()

        three = ExitStack()
        wo_hi0 = sb("wo_hi0", [P, KC, HALF], F32R, stack=three)
        wo_lo0 = sb("wo_lo0", [P, KC, HALF], F32R, stack=three)
        wo_hi1 = sb("wo_hi1", [P, KC, HALF], F32R, stack=three)
        wo_lo1 = sb("wo_lo1", [P, KC, HALF], F32R, stack=three)
        skip = sb("skip", [P, SKIP_SLOTS, D], stack=three)
        stats2 = sb("stats2", [P, T_TILES, 4, 6], stack=three)
        mv2 = sb("mv2", [P, T_TILES, 2], stack=three)
        small2 = sb("small2", [P, 8, T_TILES], stack=three)
        three.close()
        wo_hi, wo_lo = (wo_hi0, wo_hi1), (wo_lo0, wo_lo1)
        gain1, bias1 = (merged[:, n, :] for n in range(2))
        res = merged[:, 2:4, :]
        skip_dram = nc.dram_tensor("skip_dram", (T_TILES, P, D), F32, kind="Internal").ap()

        PS = ctx.enter_context(nc.psum_tensor("PS", [P, 8, HALF], F32))
        S_PS = PS[:, 3:5, 0:2 * KEYS]
        PT_PS = PS[:, 5, :].rearrange("p (g r) -> p g r", g=2)
        PTM_PS = PS[0:2 * META, 6, 0:2 * P]
        O_PS = PS[:, 7, 0:4 * CHUNK].rearrange("p (t q) -> p t q", t=4)
        STACK = tuple(slice(2 * META * n, 2 * META * (n + 1)) for n in range(3))
        META_COLS = slice(2 * CHUNK, 2 * CHUNK + 2 * META)
        WIN_COLS = (slice(0, 2 * CHUNK), slice(KEYS + META, 2 * KEYS))

        x_loaded = [sem(f"x_loaded{n}") for n in range(1 + T_TILES)]
        x0_left_loaded = sem("x0_left_loaded")
        params_loaded = sem("params_loaded")
        sinks_loaded = sem("sinks_loaded")
        pool_w_loaded = sem("pool_w_loaded")
        raw_loaded = [sem(f"raw_loaded{s}") for s in range(2)]
        ident_ready = sem("ident_ready")
        zeroed = sem("zeroed")
        params_turned = sem("params_turned")
        params_ready = sem("params_ready")
        dve_step = sem("dve_step")
        var_ready = sem("var_ready")
        root_ready = sem("root_ready")
        rstd_ready = sem("rstd_ready")
        z_by_act = sem("z_by_act")
        z_by_dve = sem("z_by_dve")
        z_turned = sem("z_turned")
        hf_by_act = sem("hf_by_act")
        hf_by_dve = sem("hf_by_dve")
        hfm_ready = sem("hfm_ready")
        h_hi_ready = sem("h_hi_ready")
        h_lo_by_pool = sem("h_lo_by_pool")
        h_lo_by_dve = sem("h_lo_by_dve")
        meta_lo_ready = sem("meta_lo_ready")
        w_hi_ready = sem("w_hi_ready")
        w_lo_ready = sem("w_lo_ready")
        groups_done = sem("groups_done")
        bank_read = [sem(f"bank_read{b}") for b in range(4)]
        v_turned = sem("v_turned")
        k_hi_ready = sem("k_hi_ready")
        v_hi_ready = sem("v_hi_ready")
        v_win_ready = sem("v_win_ready")
        v_meta_ready = sem("v_meta_ready")
        meta_staged = sem("meta_staged")
        qk_staged = sem("qk_staged")
        q_lo_staged = sem("q_lo_staged")
        v_staged = sem("v_staged")
        scores_done = sem("scores_done")
        neg_m_ready = sem("neg_m_ready")
        sink_m_ready = sem("sink_m_ready")
        probs_ready = sem("probs_ready")
        sink_e_ready = sem("sink_e_ready")
        probs_scaled = sem("probs_scaled")
        probs_turned = sem("probs_turned")
        pT_hi_ready = sem("pT_hi_ready")
        pT_ready = sem("pT_ready")
        pT_meta_hi_ready = sem("pT_meta_hi_ready")
        pT_meta_hi_copied = sem("pT_meta_hi_copied")
        pT_meta_ready = sem("pT_meta_ready")
        o_done = sem("o_done")
        o_ready = sem("o_ready")
        conv_ready = sem("conv_ready")
        conv_step = sem("conv_step")
        pool_step = sem("pool_step")
        pooled_ready = sem("pooled_ready")
        y_f_ready = sem("y_f_ready")
        gate_bias_ready = sem("gate_bias_ready")
        y_hi_ready = sem("y_hi_ready")
        y_lo_ready = sem("y_lo_ready")
        merged_step = sem("merged_step")
        m_hi_ready = sem("m_hi_ready")
        m_lo_ready = sem("m_lo_ready")
        wo_hi_ready = sem("wo_hi_ready")
        wo_lo_ready = sem("wo_lo_ready")
        rows0_loaded = sem("rows0_loaded")
        rows1_loaded = sem("rows1_loaded")
        rows0_scaled = sem("rows0_scaled")
        skip_step = sem("skip_step")
        skip_ready = sem("skip_ready")
        skip_stored = [sem(f"skip_stored{n}") for n in range(2)]
        skip_loaded = [sem(f"skip_loaded{s}") for s in range(SKIP_SLOTS)]
        out_done = sem("out_done")
        res_half = sem("res_half")
        var2_ready = sem("var2_ready")
        root2_ready = sem("root2_ready")
        mean_ready = sem("mean_ready")
        row_ready = sem("row_ready")
        stored = [sem(f"stored{s}") for s in range(2)]

        def wait_hf(eng, n):
            if n in HF_ON_DVE:
                eng.wait_ge(hf_by_dve, HF_ON_DVE.index(n) + 1)
            else:
                eng.wait_ge(hf_by_act, n + 1 - sum(m < n for m in HF_ON_DVE))

        def wait_lo(eng, n):
            if n in LO_ON_DVE:
                eng.wait_ge(h_lo_by_dve, LO_ON_DVE.index(n) + 1)
            else:
                eng.wait_ge(h_lo_by_pool, n + 1 - sum(m < n for m in LO_ON_DVE))

        def wait_h_half(eng, half):
            for n in (KC * half + KC - 2, KC * half + KC - 1):
                wait_lo(eng, n)

        def block_cols(n):
            return slice(META + HALF * (n // KC), META + HALF * (n // KC) + HALF)

        def two_turns(eng, body, apart):
            if apart:
                body(0)
                body(1)
            else:
                with eng.Fori(0, 2) as i:
                    body(i)

        block = ctx.enter_context(nc.Block())

        w_view = w_in[0].rearrange("(k p) n -> p k n", p=P)

        def token_col(t):
            return t if t < META else t + PAD

        def kv_parts(a, b):
            if a < META:
                return ((0, META - a, token_col(a)), (META - a, b - a, token_col(META)))
            return ((0, b - a, token_col(a)),)

        def raw_count(tile, slot):
            return tile * 16 + (32 - 16 * slot)

        @block.sync
        def _(sp):
            x_rows = x[0].rearrange("(t p) d -> t p d", p=P)
            for part, loaded in ((slice(0, HALF), x0_left_loaded), (slice(HALF, D), x_loaded[0])):
                sp.dma_start(xin[:, 0, part], x_rows[0][:, part]).then_inc(loaded, 16)
            for t in range(1, 4):
                sp.dma_start(xin[:, t, :], x_rows[t]).then_inc(x_loaded[t], 16)
            for row, src in ((ROW_G0, ln0_g.rearrange("(r c) -> r c", c=P)),
                             (ROW_B0, ln0_b.rearrange("(r c) -> r c", c=P)),
                             (ROW_BG, b_gate[0].rearrange("(r c) -> r c", c=P)),
                             (ROW_CONV, conv_w[0].rearrange("j (r c) -> (j r) c", c=P)),
                             (ROW_PS, pool_scale[0].rearrange("(r c) -> r c", c=P))):
                sp.dma_start(prow[row:row + src.shape[0], :], src).then_inc(params_loaded, 16)

            def load_columns(tile, slot, col):
                raw_free(tile)
                for k in (4, 0):
                    sp.dma_start(raw[:, slot, k:k + 4, :], w_view[:, k:k + 4, bass.ds(col, P)])\
                        .then_inc(raw_loaded[slot], 16)

            def load_heads(tile, slot, col):
                raw_free(tile)
                for half in range(2):
                    sp.dma_start(raw[:, slot, :, HEAD * half:HEAD * (half + 1)],
                                 w_view[:, :, bass.ds(col + 256 * half, HEAD)])\
                        .then_inc(raw_loaded[slot], 16)

            def raw_free(tile):
                if isinstance(tile, int) and tile < 2:
                    return
                sp.wait_ge(w_hi_ready, tile - 1)
                sp.wait_ge(w_lo_ready, tile - 1)

            def load_q(i, n):
                load_heads(Q.tile(i, n), n, i * (2 * HEAD) + (COL_Q + HEAD * n))

            load_q(0, 0)
            for t in range(4, T_TILES):
                sp.dma_start(xin[:, t, :], x_rows[t]).then_inc(x_loaded[t], 16)
            load_q(0, 1)
            sp.dma_start(xmeta, meta_tokens).then_inc(x_loaded[META_COL], 16)
            for dst, src in ((gain0, ln0_g), (bias0, ln0_b)):
                sp.dma_start(dst, src.rearrange("(a n) -> a n", a=1).partition_broadcast(P))\
                    .then_inc(rows0_loaded, 16)
            sp.dma_start(all_sinks[:], attn_sinks[0:1, :].partition_broadcast(P)).then_inc(sinks_loaded, 16)
            sp.dma_start(pool_wt[:], pool_w[0].rearrange("g c d -> c g d")).then_inc(pool_w_loaded, 16)
            for n in range(2):
                load_q(1, n)
            load_columns(KV.tile(0, 0), 0, COL_K)
            load_columns(KV.tile(0, 1), 1, COL_V)

            def load_mix(i, keep_skip=False):
                for n, col in enumerate((COL_CU, COL_AC, COL_AH, COL_AB)):
                    load_columns(MIX.tile(i, n), n % 2, i * P + col)
                    if keep_skip and n < 2:
                        for m in range(4 * n, 4 * n + 4):
                            t = SKIP_ORDER[m]
                            sp.wait_ge(skip_ready, m + 1)
                            sp.dma_start(skip_dram[t], xin[:, t, :]).then_inc(skip_stored[n], 16)

            load_mix(0, keep_skip=True)
            with sp.Fori(1, 4) as i:
                load_mix(i)
            for b, (col_z, w_br) in enumerate(((COL_AZ, w_br_a), (COL_BZ, w_br_b), (COL_CZ, w_br_c))):
                with sp.Fori(0, 2) as i:
                    for n in range(2):
                        if b == 1:
                            load_heads(Z[b].tile(i, n), n, i * (2 * HEAD) + (col_z + HEAD * n))
                        else:
                            load_columns(Z[b].tile(i, n), n, i * (2 * P) + (col_z + P * n))
                with sp.Fori(0, 2) as i:
                    for pair in range(2):
                        for n in range(2):
                            tile = GATE[b].tile(i, 3 * pair + n)
                            load_columns(tile, (3 * pair + n) % 2,
                                         i * (4 * P) + (COL_GATE + D * b + P * (2 * pair + n)))
                        n = 3 * pair + 2
                        raw_free(GATE[b].tile(i, n))
                        dst = raw[:, n % 2, :, :].rearrange("p (k two) c -> p k (two c)", two=2)
                        for half in (1, 0):
                            rows = (w_br[0, 256 * half:256 * half + 256, :].rearrange("(k p) n -> p k n", p=64)
                                    if b == 1 else
                                    w_br[0].rearrange("(k p) n -> p k n", p=P)[64 * half:64 * half + 64])
                            sp.dma_start(dst[64 * half:64 * half + 64],
                                         rows[:, :, bass.ds(i * (4 * P) + 2 * P * pair, 2 * P)])\
                                .then_inc(raw_loaded[n % 2], 16)
            wo_view = w_out[0].rearrange("(k p) n -> p k n", p=P)
            for n in range(OUT_PIECES):
                half, k = n // 4, 2 * (n % 4)
                if n < 2:
                    raw_free(N_TILES + n)
                else:
                    sp.wait_ge(wo_hi_ready, n - 1)
                    sp.wait_ge(wo_lo_ready, n - 1)
                dst = raw[:, n % 2, :, :].rearrange("p (k four) c -> p k (four c)", four=4)
                for j in range(2):
                    sp.dma_start(dst[:, j, :], wo_view[:, k + j, HALF * half:HALF * half + HALF])\
                        .then_inc(raw_loaded[n % 2], 16)
            sp.wait_ge(m_hi_ready, 2 * KC)
            sp.wait_ge(m_lo_ready, 2 * KC)
            for dst, src in ((gain1, ln_g[0]), (bias1, ln_b[0])):
                sp.dma_start(dst, src.rearrange("(a n) -> a n", a=1).partition_broadcast(P))\
                    .then_inc(rows1_loaded, 16)
            out_rows = out[0].rearrange("(t p) d -> t p d", p=P)

            def load_skip(t):
                sp.dma_start(skip[:, t % SKIP_SLOTS, :], skip_dram[t])\
                    .then_inc(skip_loaded[t % SKIP_SLOTS], 16)

            for n in range(2):
                sp.wait_ge(skip_stored[n], 16 * 4)
            for t in range(SKIP_SLOTS):
                load_skip(t)
            for t in range(T_TILES):
                if t + SKIP_SLOTS < T_TILES:
                    sp.wait_ge(res_half, 2 * t + 2)
                    load_skip(t + SKIP_SLOTS)
                for part in ((0, D),) if t < T_TILES - 1 else ((0, HALF), (HALF, D)):
                    cols = slice(*part)
                    sp.wait_ge(row_ready, t + 1 + (part[0] > 0))
                    sp.dma_start(out_rows[t][:, cols], res[:, t % 2, cols]).then_inc(stored[t % 2], 16)
            for s in range(2):
                sp.wait_ge(stored[s], 16 * (T_TILES // 2 + s))

        @block.gpsimd
        def _(pool):
            g = nc.gpsimd
            g.memset(ident[:], 0.0).then_inc(ident_ready, 1)
            g.memset(mv[:], 1.0).then_inc(zeroed, 1)
            pool.wait_ge(ident_ready, 1)
            g.affine_select(out=ident[:], in_=ident[:], compare_op=ALU.not_equal, fill=1.0, base=0,
                            pattern=[[-1, P]], channel_multiplier=1).then_inc(ident_ready, 1)
            g.memset(kT[:, :, META:META + PAD].bitcast(F32), 0.0).then_inc(zeroed, 1)
            g.memset(vT[:, META:META + PAD], 0.0).then_inc(zeroed, 1)
            g.memset(k_stage[:].bitcast(F32), 0.0).then_inc(zeroed, 1)
            g.memset(v_stage[:].bitcast(F32), 0.0).then_inc(zeroed, 1)
            g.memset(vT_meta_bd[:], 0.0).then_inc(zeroed, 1)
            pool.wait_ge(raw_loaded[0], raw_count(0, 0))
            pool.wait_ge(w_hi_ready, 1)
            g.tensor_tensor(w_lo[:, 0], raw[:, 0], w_hi[:, 0].bitcast(F32), ALU.subtract).then_inc(w_lo_ready, 1)
            for n in range(2 * KC):
                if n not in LO_ON_DVE:
                    pool.wait_ge(h_hi_ready, n + 1)
                    cols = block_cols(n)
                    g.tensor_tensor(h_lo[:, n % KC, cols], hf[:, n % 4, :], h_hi[:, n % KC, cols].bitcast(F32),
                                    ALU.subtract).then_inc(h_lo_by_pool, 1)

            pool.wait_ge(rows0_scaled, 2)
            pool.wait_ge(z_turned, 2 * KC)
            for n, t in enumerate(SKIP_ORDER):
                if n == 2:
                    pool.wait_ge(h_hi_ready, 2 * KC + 1)
                    g.tensor_tensor(h_lo[:, :, 0:META], hfm, h_hi[:, :, 0:META].bitcast(F32), ALU.subtract)\
                        .then_inc(meta_lo_ready, 1)
                g.tensor_tensor(xin[:, t, :], xin[:, t, :], gain0, ALU.mult).then_inc(skip_step, 1)
                pool.wait_ge(skip_step, n + 1)
                g.tensor_tensor(xin[:, t, :], xin[:, t, :], bias0, ALU.add).then_inc(skip_ready, 1)
            pool.wait_ge(skip_ready, T_TILES)

            step = 0
            for i, w in enumerate(POOL_WINDOWS):
                for n in range(3):
                    pool.wait_ge(bank_read[MIX.banks[n]], MIX.used(i, n) + 1)
                src, size = cu_sb, 1
                for dst in (win_a, win_b, win_a, win_b)[:i + 1]:
                    lead = 2 * size - 1
                    g.tensor_tensor(dst[:, lead:TOK], src[:, lead:TOK], src[:, lead - size:TOK - size],
                                    ALU.add).then_inc(pool_step, 1)
                    step += 1
                    pool.wait_ge(pool_step, step)
                    src, size = dst, 2 * size
                g.tensor_scalar(src[:, META:TOK], src[:, META:TOK], 1.0 / w, None, ALU.mult)\
                    .then_inc(pool_step, 1)
                step += 1
                pool.wait_ge(pool_step, step)
                g.tensor_tensor(pooled[:, i, :], src[:, META:TOK], cu_sb[:, META:TOK], ALU.subtract)\
                    .then_inc(pooled_ready, 1)

        def split_hi(act, tile, slot, groups_before):
            n = tile // 2 if isinstance(tile, int) else None
            act.wait_ge(raw_loaded[slot], raw_count(tile, slot))
            if groups_before is not None:
                act.wait_ge(groups_done, groups_before)
            nc.scalar.activation(w_hi[:, slot], raw[:, slot], ACT.Copy).then_inc(w_hi_ready, 1)

        def split_lo(dve, tile, slot, groups_before):
            dve.wait_ge(raw_loaded[slot], raw_count(tile, slot))
            dve.wait_ge(w_hi_ready, tile + 1)
            if groups_before is not None:
                dve.wait_ge(groups_done, groups_before)
            nc.vector.tensor_tensor(w_lo[:, slot], raw[:, slot], w_hi[:, slot].bitcast(F32),
                                    ALU.subtract).then_inc(w_lo_ready, 1)

        def split_next(eng, split, sec, turn, n, g):
            split(eng, sec.tile(turn, n) + 1, (n + 1) % 2, sec.groups(turn, g))

        def out_part(parts, n):
            half, k = n // 4, 2 * (n % 4)
            return (parts[half][:, k:k + 2, :],
                    raw[:, n % 2, :, :].rearrange("p (k four) c -> p k (four c)", four=4))

        def split_out_hi(act, n):
            act.wait_ge(raw_loaded[n % 2], raw_count(N_TILES + n, n % 2))
            dst, src = out_part(wo_hi, n)
            nc.scalar.activation(dst, src, ACT.Copy).then_inc(wo_hi_ready, 1)

        def split_out_lo(dve, n):
            dve.wait_ge(raw_loaded[n % 2], raw_count(N_TILES + n, n % 2))
            dve.wait_ge(wo_hi_ready, n + 1)
            dst, src = out_part(wo_lo, n)
            hi, _ = out_part(wo_hi, n)
            nc.vector.tensor_tensor(dst, src, hi.bitcast(F32), ALU.subtract).then_inc(wo_lo_ready, 1)

        def m_cols(c):
            return slice(META + HALF * c, META + HALF * c + HALF)

        def split_m_hi(act, j, c):
            act.wait_ge(merged_step, 16 * (N_BRANCH - 1) + 2 * j + c + 1)
            act.wait_ge(groups_done, H_LAST_GROUP)
            nc.scalar.activation(h_hi[:, j, m_cols(c)], merged[:, j, HALF * c:HALF * c + HALF], ACT.Copy)\
                .then_inc(m_hi_ready, 1)

        def split_m_lo(dve, j, c):
            dve.wait_ge(m_hi_ready, KC * c + j + 1)
            nc.vector.tensor_tensor(h_lo[:, j, m_cols(c)], merged[:, j, HALF * c:HALF * c + HALF],
                                    h_hi[:, j, m_cols(c)].bitcast(F32), ALU.subtract).then_inc(m_lo_ready, 1)

        def out_bank(t, h):
            return (4 + 2 * t + h) % 8

        def out_parts(t):
            return ((0, HALF), (HALF, D)) if t < T_TILES - 1 else ((0, HALF), (HALF, D - HALF // 2),
                                                                  (D - HALF // 2, D))

        def part_bank(t, n):
            return (out_bank(t, 0) + n) % 8

        def out_count(t, h):
            return SIDE * h + t + 1 if t < SIDE else 2 * t + h + 1

        V_BANKS = (2, 5, 6, 7)
        STAT_BATCHES = (slice(0, 4), slice(4, 8), slice(8, 9))

        @block.scalar
        def _(act):
            s = nc.scalar

            def root(n):
                act.wait_ge(var_ready, n + 1)
                cols = STAT_BATCHES[n]
                s.activation(small[:, 0, cols], mv[:, cols, 1], ACT.Sqrt).then_inc(root_ready, 1)

            def normalise(c):
                part = xmeta if c == META_COL else xin[:, c, :]
                rows = META if c == META_COL else P
                s.activation(part, part, ACT.Identity, bias=nmr[0:rows, c:c + 1], scale=rstd[0:rows, c:c + 1])\
                    .then_inc(z_by_act, 1)

            def h_block(n):
                if n < 2 * KC and n not in HF_ON_DVE:
                    act.wait_ge(z_turned, n + 1)
                    if n >= 4:
                        wait_lo(act, n - 4)
                    s.activation(hf[:, n % 4, :], PS[:, 3 + n % 4, :], ACT.Identity,
                                 bias=column(ROW_B0 + n % KC), scale=column(ROW_G0 + n % KC))\
                        .then_inc(hf_by_act, 1)
                m = n - 1
                if n % KC:
                    h_hi_block(m)

            def h_hi_block(m):
                wait_hf(act, m)
                s.activation(h_hi[:, m % KC, block_cols(m)], hf[:, m % 4, :], ACT.Copy).then_inc(h_hi_ready, 1)

            root(0)
            act.wait_ge(rstd_ready, 1)
            normalise(0)
            normalise(1)
            split_hi(act, 0, 0, None)
            act.wait_ge(params_ready, 1)
            for n in range(KC):
                h_block(n)
                if n == 3:
                    root(1)
                if n == 5:
                    split_hi(act, 1, 1, None)
            h_hi_block(KC - 1)
            for n in range(KC, 2 * KC):
                h_block(n)
            h_hi_block(2 * KC - 1)

            def read_group(sec, turn, g, dst, func=ACT.Copy, src_cols=None, last=True, **kw):
                b = sec.banks[g]
                a, z = src_cols
                act.wait_ge(groups_done, sec.groups(turn, g) + 1)
                ins = s.activation(dst, PS[:, b, a:z], func, **kw)
                if last:
                    ins.then_inc(bank_read[b], 1)

            wait_h_half(act, 1)
            for i in range(2):
                if i == 1:
                    split_hi(act, Q.tile(1, 1), 1, Q.groups(1, 0))
                for g in range(4):
                    n, c = g % 2, g // 2
                    if g == 3:
                        split_hi(act, Q.tile(i, 2), 0, Q.groups(i, 3))
                    read_group(Q, i, g, q_o[:, 2 * i + n, HALF * c:HALF * c + HALF], src_cols=(0, HALF))
                    if i == 0 and g == 1:
                        root(2)
                        act.wait_ge(rstd_ready, 3)
                        normalise(META_COL)
                if i == 0:
                    act.wait_ge(hfm_ready, 1)
                    s.activation(h_hi[:, :, 0:META], hfm, ACT.Copy).then_inc(h_hi_ready, 1)

            def stage_qk(i, n):
                chunk = i * 4 + n
                wait(act, scores_done, chunk)
                s.activation(q_stage[:, 0], q_o[:, :, bass.ds(chunk * CHUNK, CHUNK)], ACT.Copy)\
                    .then_inc(qk_staged, 1)
                for g in range(2):
                    rows = slice(64 * g, 64 * g + 64)
                    s.activation(k_stage[rows, :, WIN_COLS[g]],
                                 kT[rows, :, bass.ds(chunk * CHUNK + META, 2 * CHUNK)], ACT.Copy)\
                        .then_inc(qk_staged, 1)

            def stage_v(i, n):
                chunk = i * 4 + n
                wait(act, o_done, chunk)
                for g in range(2):
                    s.activation(v_stage[:, :, 2 * g, :],
                                 v_win[:, :, bass.ds(chunk, 1), HEAD * g:HEAD * g + HEAD]
                                 .rearrange("p h w d -> p h (w d)"), ACT.Copy).then_inc(v_staged, 1)

            def softmax_exp(i, n):
                chunk = i * 4 + n
                act.wait_ge(neg_m_ready, chunk + 1)
                wait(act, probs_turned, chunk)
                for c in range(2):
                    for g in range(2):
                        j, cols = 2 * c + g, slice(KEYS * g, KEYS * g + KEYS)
                        s.activation(probs[:, c, cols], S_PS[:, c, cols], ACT.Exp,
                                     bias=neg_m[:, j:j + 1], scale=SCALE, accum_out=row_sum[:, j:j + 1])\
                            .then_inc(probs_ready, 1)
                act.wait_ge(sink_m_ready, chunk + 1)
                s.activation(sink_e, sink_m, ACT.Exp).then_inc(sink_e_ready, 1)

            def copy_pT_meta(i, n):
                chunk = i * 4 + n
                act.wait_ge(probs_turned, chunk + 1)
                wait(act, o_done, chunk)
                s.activation(pT_meta[STACK[0], :], PTM_PS, ACT.Copy).then_inc(pT_meta_hi_ready, 1)
                act.wait_ge(pT_meta_hi_ready, chunk + 1)
                s.activation(pT_meta[STACK[2], :], pT_meta[STACK[0], :], ACT.Copy)\
                    .then_inc(pT_meta_hi_copied, 1)

            act.wait_ge(zeroed, N_ZEROED)
            for n in range(2):
                split_next(act, split_hi, KV, 0, n, 3 * n)
                for c, (a, b) in enumerate(WITH_META):
                    parts = kv_parts(a, b)
                    for m, (p0, p1, col) in enumerate(parts):
                        if n == 0:
                            act.wait_ge(groups_done, KV.groups(0, c) + 1)
                            s.activation(kT[:, 0, col:col + p1 - p0], PS[:, KV.banks[c], p0:p1], ACT.Copy)\
                                .then_inc(k_hi_ready, 1)
                        else:
                            read_group(KV, 0, 3 * n + c, vT[:, col:col + p1 - p0], src_cols=(p0, p1),
                                       last=m == len(parts) - 1)
                    if c == 0:
                        for b in range(3) if n else (0,):
                            act.wait_ge(bank_read[b], KV.used_end[b] - 1 + (n and b == 0))
                        for g in range(2):
                            rows, cols = slice(64 * g, 64 * g + 64), slice(META * g, META * g + META)
                            if n == 0:
                                at = META_COLS.start + META * g
                                s.activation(k_stage[rows, :, at:at + META], kT[rows, :, 0:META], ACT.Copy)\
                                    .then_inc(meta_staged, 1)
                            else:
                                s.activation(vT_meta_bd[rows, cols], vT[rows, 0:META], ACT.Copy)\
                                    .then_inc(meta_staged, 1)
                        if n == 1:
                            stage_qk(0, 0)

            def mix_turn(i, first=False):
                if not first:
                    stage_qk(i, 0)
                split_next(act, split_hi, MIX, i, 0, 0)
                for g in range(11):
                    tile, c = min(g // 3, 3), g - 3 * min(g // 3, 3)
                    if c == 0 and tile > 0:
                        split_next(act, split_hi, MIX, i, tile, g)
                    if tile < 2:
                        a, b = (WITH_META, FOR_CONV)[tile][c]
                        act.wait_ge(groups_done, MIX.groups(i, g) + 1)
                        if tile == 0:
                            wait(act, pooled_ready, i)
                        else:
                            wait(act, conv_ready, i)
                        read_group(MIX, i, g, (cu_sb, ac_sb)[tile][:, a:b], src_cols=(0, b - a))
                    if g in TURN_AFTER:
                        if first and g == TURN_AFTER[0]:
                            act.wait_ge(v_win_ready, 4)
                        stage_v(i, TURN_AFTER.index(g))
                        copy_pT_meta(i, TURN_AFTER.index(g))
                    if first and g == 0:
                        act.wait_ge(skip_stored[0], 16 * 4)
                        for n, bank in enumerate(V_BANKS):
                            act.wait_ge(v_turned, n + 1)
                            s.activation(v_win[:, 0, 4 * n:4 * n + 4, :],
                                         PS[:, bank, :].rearrange("p (w c) -> p w c", w=4), ACT.Copy)\
                                .then_inc(v_hi_ready, 1)
                    if g in SCORES_AFTER:
                        n = SCORES_AFTER.index(g)
                        softmax_exp(i, n)
                        if n < 3:
                            stage_qk(i, n + 1)

            mix_turn(0, first=True)
            with act.Fori(1, 4) as i:
                mix_turn(i)

            for b in range(N_BRANCH):
                def z_turn(i):
                    for n in range(2):
                        split_next(act, split_hi, Z[b], i, n, 2 * n)
                        k = i * 2 + n
                        for c in range(2):
                            g = 2 * n + c
                            act.wait_ge(groups_done, Z[b].groups(i, g) + 1)
                            wait(act, y_f_ready, k * 2 + (8 * b + c - 1))
                            read_group(Z[b], i, g, silu[:, c, :], ACT.Silu, src_cols=(0, HALF))
                        for c in range(2):
                            act.wait_ge(y_f_ready, k * 2 + (8 * b + c + 1))
                            s.activation(y_hi[:, bass.ds(k, 1), HALF * c:HALF * c + HALF],
                                         y_f[:, bass.ds(c, 1), :], ACT.Copy).then_inc(y_hi_ready, 1)
                two_turns(act, z_turn, apart=b == 0)

                def gate_turn(i):
                    wait(act, merged_step, i * 8 + 16 * b)
                    s.activation(gate_bias[:], params[:, bass.ds(i * 4 + (ROW_BG + 8 * b), 4)], ACT.Copy)\
                        .then_inc(gate_bias_ready, 1)
                    act.wait_ge(gate_bias_ready, i + (2 * b + 1))
                    for pair in range(2):
                        last_pair = b == N_BRANCH - 1 and isinstance(i, int) and i == 1 and pair == 1
                        for n in range(2):
                            tile, g = 3 * pair + n, 8 * pair + 2 * n
                            split_next(act, split_hi, GATE[b], i, tile, g)
                            if last_pair and n == 1:
                                for piece in range(2):
                                    split_out_hi(act, piece)
                            for c in range(2):
                                act.wait_ge(groups_done, GATE[b].groups(i, g + c) + 1)
                                wait(act, merged_step, i * 8 + (16 * b + 4 * pair))
                                s.activation(sig[:, n, HALF * c:HALF * c + HALF], PS[:, GATE[b].banks[g + c], :],
                                             ACT.Sigmoid,
                                             bias=gate_bias[:, 2 * pair + n:2 * pair + n + 1])\
                                    .then_inc(bank_read[GATE[b].banks[g + c]], 1)
                        if not last_pair:
                            split_next(act, split_hi, GATE[b], i, 3 * pair + 2, 8 * pair + 4)

                two_turns(act, gate_turn, apart=b != 1)

            for piece in range(2, 4):
                split_out_hi(act, piece)
            for j in range(KC):
                split_m_hi(act, j, 0)
            act.wait_ge(groups_done, GROUPS_IN)
            for piece in range(4, OUT_PIECES):
                split_out_hi(act, piece)
            for j in range(KC):
                split_m_hi(act, j, 1)

            for t in range(T_TILES):
                act.wait_ge(var2_ready, t + 1)
                s.activation(small2[:, 1, t:t + 1], small2[:, 0, t:t + 1], ACT.Sqrt).then_inc(root2_ready, 1)

        @block.vector
        def _(dve):
            v = nc.vector
            steps = [0]

            def then(ins):
                ins.then_inc(dve_step, 1)
                steps[0] += 1
                dve.wait_ge(dve_step, steps[0])

            def rsqrt(var, root, r, a):
                then(v.reciprocal(r, root))
                then(v.scalar_tensor_tensor(a, r, -0.5, r, ALU.mult, ALU.mult))
                then(v.tensor_tensor(a, a, var, ALU.mult))
                then(v.scalar_tensor_tensor(r, a, 1.5, r, ALU.add, ALU.mult))

            def row_stats(c):
                dve.wait_ge(x0_left_loaded if c == 0 else x_loaded[c], 16)
                rows = META if c == META_COL else P
                part = xmeta if c == META_COL else xin[:, c, :]
                v.bn_stats(stats[0:rows, c, 0, :], part[:, 0:HALF]).then_inc(dve_step, 1)
                if c == 0:
                    dve.wait_ge(x_loaded[0], 16)
                v.bn_stats(stats[0:rows, c, 1, :], part[:, HALF:D]).then_inc(dve_step, 1)
                steps[0] += 2
                dve.wait_ge(dve_step, steps[0])
                then(v.bn_aggr(mv[0:rows, c, :], stats[0:rows, c, :, :]))

            def row_rstd(n, meanwhile=None):
                cols = STAT_BATCHES[n]
                v.tensor_scalar(mv[:, cols, 1], mv[:, cols, 1], LN_EPS, None, ALU.add).then_inc(var_ready, 1)
                if meanwhile:
                    meanwhile()
                dve.wait_ge(root_ready, n + 1)
                rsqrt(mv[:, cols, 1], small[:, 0, cols], rstd[:, cols], small[:, 1, cols])
                v.scalar_tensor_tensor(nmr[:, cols], mv[:, cols, 0], -1.0, rstd[:, cols], ALU.mult, ALU.mult)\
                    .then_inc(rstd_ready, 1)

            def normalise(c):
                v.tensor_scalar(xin[:, c, :], xin[:, c, :], rstd[:, c:c + 1], nmr[:, c:c + 1],
                                ALU.mult, ALU.add).then_inc(z_by_dve, 1)

            def copy_params():
                dve.wait_ge(params_turned, 1)
                v.tensor_copy(params[:], PS[:, 7, 0:N_ROWS]).then_inc(params_ready, 1)

            def hf_block(n):
                dve.wait_ge(z_turned, n + 1)
                wait_lo(dve, n - 4)
                v.tensor_scalar(hf[:, n % 4, :], PS[:, 3 + n % 4, :], column(ROW_G0 + n % KC),
                                column(ROW_B0 + n % KC), ALU.mult, ALU.add).then_inc(hf_by_dve, 1)

            def lo_block(n):
                dve.wait_ge(h_hi_ready, n + 1)
                cols = block_cols(n)
                v.tensor_tensor(h_lo[:, n % KC, cols], hf[:, n % 4, :], h_hi[:, n % KC, cols].bitcast(F32),
                                ALU.subtract).then_inc(h_lo_by_dve, 1)

            dve.wait_ge(zeroed, 1)
            for c in range(4):
                row_stats(c)
            row_rstd(0, meanwhile=copy_params)
            dve.wait_ge(rstd_ready, 1)
            normalise(2)
            normalise(3)
            for c in range(4, 8):
                row_stats(c)

            dve.wait_ge(params_ready, 1)
            row_rstd(1, meanwhile=lambda: hf_block(HF_ON_DVE[0]))
            dve.wait_ge(rstd_ready, 2)
            for c in range(4, 8):
                normalise(c)
            lo_block(7)
            split_lo(dve, 1, 1, None)
            for n in HF_ON_DVE[1:]:
                hf_block(n)
                lo_block(n)
            row_stats(META_COL)
            row_rstd(2)
            dve.wait_ge(rows0_loaded, 32)
            for row in (gain0, bias0):
                v.tensor_scalar(row, row, ALPHA, None, ALU.mult).then_inc(rows0_scaled, 1)
            dve.wait_ge(z_turned, 2 * KC + 1)
            zm = PS[:, 7, P:2 * P].rearrange("p (k m) -> p k m", m=META)
            gain = params[:, ROW_G0:ROW_G0 + KC].unsqueeze(2).to_broadcast([P, KC, META])
            bias = params[:, ROW_B0:ROW_B0 + KC].unsqueeze(2).to_broadcast([P, KC, META])
            then(v.tensor_tensor(hfm, zm, gain, ALU.mult))
            v.tensor_tensor(hfm, hfm, bias, ALU.add).then_inc(hfm_ready, 1)

            dve.wait_ge(sinks_loaded, 16)
            for e in range(2):
                rows = slice(64 * e, 64 * e + 64)
                then(v.tensor_copy(sink[rows, :].rearrange("p (c g) -> p c g", c=2),
                                   all_sinks[rows, :].rearrange("p (g c e) -> p c g e", g=2, c=2)[:, :, :, e]))
            then(v.tensor_scalar(neg_sink[:], sink[:], -1.0, None, ALU.mult))

            split_lo(dve, Q.tile(0, 2), 0, Q.groups(0, 3))
            split_lo(dve, Q.tile(1, 1), 1, Q.groups(1, 0))
            split_lo(dve, Q.tile(1, 2), 0, Q.groups(1, 3))
            split_next(dve, split_lo, KV, 0, 0, 0)
            n_parts = 0
            for c, (a, b) in enumerate(WITH_META):
                parts = kv_parts(a, b)
                n_parts += len(parts)
                dve.wait_ge(k_hi_ready, n_parts)
                for m, (p0, p1, col) in enumerate(parts):
                    cols = slice(col, col + p1 - p0)
                    ins = v.tensor_tensor(kT[:, 1, cols], PS[:, KV.banks[c], p0:p1], kT[:, 0, cols].bitcast(F32),
                                          ALU.subtract)
                ins.then_inc(bank_read[KV.banks[c]], 1)
            split_next(dve, split_lo, KV, 0, 1, 3)

            def v_windows_lo():
                for n, bank in enumerate(V_BANKS):
                    dve.wait_ge(v_hi_ready, n + 1)
                    v.tensor_tensor(v_win[:, 1, 4 * n:4 * n + 4, :],
                                    PS[:, bank, :].rearrange("p (w c) -> p w c", w=4),
                                    v_win[:, 0, 4 * n:4 * n + 4, :].bitcast(F32), ALU.subtract)\
                        .then_inc(v_win_ready, 1)

            def q_lo(i, n):
                chunk = i * 4 + n
                dve.wait_ge(qk_staged, chunk * 3 + 1)
                q = q_o[:].rearrange("p t (n q) -> p t n q", q=CHUNK)[:, :, bass.ds(chunk, 1), :]
                v.tensor_tensor(q_stage[:, 1], q.rearrange("p t n q -> p t (n q)"),
                                q_stage[:, 0].bitcast(F32), ALU.subtract).then_inc(q_lo_staged, 1)

            def softmax_max(i, n, first=False):
                chunk = i * 4 + n
                dve.wait_ge(scores_done, chunk + 1)
                if first:
                    for g in range(2):
                        before = slice(WIN_COLS[g].start, WIN_COLS[g].start + CHUNK)
                        then(v.memset(S_PS[:, :, before], NEG_INF / SCALE))
                then_loop(i, v.tensor_reduce(row_max.rearrange("p (c g) -> p c g", c=2),
                                             S_PS.rearrange("p c (g k) -> p c g k", g=2), AX_X, ALU.max))
                wait(dve, sink_e_ready, chunk)
                v.scalar_tensor_tensor(neg_m, row_max, -SCALE, neg_sink[:], ALU.mult, ALU.min)\
                    .then_inc(neg_m_ready, 1)
                dve.wait_ge(neg_m_ready, chunk + 1)
                v.tensor_tensor(sink_m, neg_m, sink[:], ALU.add).then_inc(sink_m_ready, 1)

            def then_loop(turn, ins):
                ins.then_inc(conv_step, 1)
                loop_steps[0] += 1
                dve.wait_ge(conv_step, turn * STEPS + loop_steps[0])

            def scale_probs(i, n):
                chunk = i * 4 + n
                dve.wait_ge(probs_ready, chunk * 4 + 4)
                dve.wait_ge(sink_e_ready, chunk + 1)
                then_loop(i, v.tensor_tensor(denom, row_sum, sink_e, ALU.add))
                then_loop(i, v.reciprocal(r_den, denom))
                p4 = probs[:].rearrange("p c (g k) -> p (c g) k", g=2)
                v.tensor_tensor(p4, p4, r_den.unsqueeze(2).to_broadcast([P, 4, KEYS]), ALU.mult)\
                    .then_inc(probs_scaled, 1)

            def copy_pT(i, n):
                chunk = i * 4 + n
                dve.wait_ge(probs_turned, chunk + 1)
                wait(dve, o_done, chunk)
                v.tensor_copy(pT[:, 0], PT_PS).then_inc(pT_hi_ready, 1)
                dve.wait_ge(pT_hi_ready, chunk + 1)
                v.tensor_tensor(pT[:, 1], PT_PS, pT[:, 0].bitcast(F32), ALU.subtract).then_inc(pT_ready, 1)
                dve.wait_ge(pT_meta_hi_ready, chunk + 1)
                v.tensor_tensor(pT_meta[STACK[1], :], PTM_PS, pT_meta[STACK[0], :].bitcast(F32), ALU.subtract)\
                    .then_inc(pT_meta_ready, 1)

            def copy_o(i, n):
                chunk = i * 4 + n
                dve.wait_ge(bank_read[0], Q.used_end[0])
                dve.wait_ge(o_done, chunk + 1)
                v.tensor_copy(q_o[:, :, bass.ds(chunk * CHUNK, CHUNK)], O_PS).then_inc(o_ready, 1)

            STEPS = 4 * 3 + 2
            loop_steps = [0]

            def mix_turn(i, first=False):
                loop_steps[0] = 0
                q_lo(i, 0)
                for g in range(11):
                    tile, c = min(g // 3, 3), g - 3 * min(g // 3, 3)
                    if g + 1 in TURN_AFTER:
                        n = TURN_AFTER.index(g + 1)
                        scale_probs(i, n)
                        if n < 3:
                            q_lo(i, n + 1)
                    if c == 0:
                        split_next(dve, split_lo, MIX, i, tile, g)
                    if tile == 2:
                        a, b = FOR_CONV[c]
                        dve.wait_ge(bank_read[MIX.banks[3 + c]], MIX.used(i, 3 + c) + 1)
                        dve.wait_ge(groups_done, MIX.groups(i, g) + 1)
                        v.tensor_tensor(u_sb[:, a:b], PS[:, MIX.banks[g], 0:b - a], ac_sb[:, a:b], ALU.mult)\
                            .then_inc(bank_read[MIX.banks[g]], 1)
                        if c == 2:
                            for j in range(3):
                                dve.wait_ge(bank_read[MIX.banks[6 + j]], MIX.used(i, 6 + j) + 1)
                            if first:
                                dve.wait_ge(skip_stored[1], 16 * 4)
                            dst = conv_out[:, bass.ds(i, 1), :]
                            u3 = u_sb[:].unsqueeze(1)
                            tap = [params[:, bass.ds(i + (ROW_CONV + 4 * j), 1)] for j in range(3)]
                            then_loop(i, v.tensor_scalar(dst, u3[:, :, META:TOK], tap[2], None, ALU.mult))
                            for back in (1, 2):
                                ins = v.scalar_tensor_tensor(dst, u3[:, :, META - back:TOK - back],
                                                             tap[2 - back], dst, ALU.mult, ALU.add)
                                if back == 1:
                                    then_loop(i, ins)
                                else:
                                    ins.then_inc(conv_ready, 1)
                    if tile == 3:
                        dve.wait_ge(groups_done, MIX.groups(i, g) + 1)
                        dve.wait_ge(conv_ready, i + 1)
                        dst = conv_out[:, bass.ds(i, 1), HALF * c:HALF * c + HALF]
                        v.tensor_tensor(dst, PS[:, MIX.banks[g]:MIX.banks[g] + 1, :], dst, ALU.mult)\
                            .then_inc(bank_read[MIX.banks[g]], 1)
                    if g in TIMES_V_AFTER:
                        copy_o(i, TIMES_V_AFTER.index(g))
                    if g in TURN_AFTER:
                        copy_pT(i, TURN_AFTER.index(g))
                    if first and g == 1:
                        dve.wait_ge(v_turned, 5)
                        for n in range(2):
                            then(v.tensor_copy(v_meta[STACK[n], :], PS[0:2 * META, 7, 0:P]))
                        v.tensor_tensor(v_meta[STACK[2], :], PS[0:2 * META, 7, 0:P],
                                        v_meta[STACK[0], :].bitcast(F32), ALU.subtract)\
                            .then_inc(v_meta_ready, 1)
                    if g in SCORES_AFTER:
                        softmax_max(i, SCORES_AFTER.index(g), first and g == SCORES_AFTER[0])
                    if first and g == 0:
                        v_windows_lo()
                assert loop_steps[0] == STEPS, loop_steps

            mix_turn(0, first=True)
            with dve.Fori(1, 4) as i:
                mix_turn(i)

            for n in range(8):
                i, c = n // 2, n % 2
                dve.wait_ge(groups_done, MAP.groups(0, n) + 1)
                v.tensor_scalar(pooled[:, i, HALF * c:HALF * c + HALF], PS[:, MAP.banks[n], :],
                                column(ROW_PS + i), None, ALU.mult).then_inc(bank_read[MAP.banks[n]], 1)

            for b in range(4):
                dve.wait_ge(bank_read[b], MAP.used_end[b])
            dve.wait_ge(o_ready, N_CHUNKS)
            for b, mixed in enumerate((conv_out, q_o, pooled)):
                def z_turn(i):
                    for n in range(2):
                        split_next(dve, split_lo, Z[b], i, n, 2 * n)
                        k = i * 2 + n
                        for c in range(2):
                            g = 2 * n + c
                            dve.wait_ge(bank_read[Z[b].banks[g]], Z[b].used(i, g) + 1)
                            wait(dve, y_hi_ready, k * 2 + (8 * b))
                            wait(dve, y_lo_ready, k * 2 + (8 * b))
                            v.tensor_tensor(y_f[:, bass.ds(c, 1), :], silu[:, bass.ds(c, 1), :],
                                            mixed[:, bass.ds(k, 1), HALF * c:HALF * c + HALF], ALU.mult)\
                                .then_inc(y_f_ready, 1)
                        for c in range(2):
                            dve.wait_ge(y_f_ready, k * 2 + (8 * b + c + 1))
                            dve.wait_ge(y_hi_ready, k * 2 + (8 * b + c + 1))
                            cols = slice(HALF * c, HALF * c + HALF)
                            v.tensor_tensor(y_lo[:, bass.ds(k, 1), cols], y_f[:, bass.ds(c, 1), :],
                                            y_hi[:, bass.ds(k, 1), cols].bitcast(F32), ALU.subtract)\
                                .then_inc(y_lo_ready, 1)
                def gate_turn(i):
                    for pair in range(2):
                        last_pair = b == N_BRANCH - 1 and isinstance(i, int) and i == 1 and pair == 1
                        for n in range(2):
                            split_next(dve, split_lo, GATE[b], i, 3 * pair + n, 8 * pair + 2 * n)
                        if last_pair:
                            for piece in range(4):
                                split_out_lo(dve, piece)
                            for j in range(KC - 2):
                                split_m_lo(dve, j, 0)
                        else:
                            split_next(dve, split_lo, GATE[b], i, 3 * pair + 2, 8 * pair + 4)
                        for n in range(2):
                            for c in range(2):
                                g, gate = 8 * pair + 4 + 2 * n + c, 8 * pair + 2 * n + c
                                bank, cols = GATE[b].banks[g], slice(HALF * c, HALF * c + HALF)
                                out_at = merged[:, bass.ds(i * 4 + (2 * pair + n), 1), cols]
                                prod = sig[:, n:n + 1, cols]
                                dve.wait_ge(groups_done, GATE[b].groups(i, g) + 1)
                                dve.wait_ge(bank_read[GATE[b].banks[gate]], GATE[b].used(i, gate) + 1)
                                v.tensor_tensor(prod, PS[:, bank:bank + 1, :], prod, ALU.mult)\
                                    .then_inc(bank_read[bank], 1)
                                dve.wait_ge(bank_read[bank], GATE[b].used(i, g) + 1)
                                if b == 0:
                                    v.tensor_copy(out_at, prod).then_inc(merged_step, 1)
                                else:
                                    v.tensor_tensor(out_at, out_at, prod, ALU.add).then_inc(merged_step, 1)
                                if last_pair and c == 0:
                                    split_m_lo(dve, KC - 2 + n, 0)

                two_turns(dve, z_turn, apart=b == 0)
                wait(dve, merged_step, 16 * b)
                two_turns(dve, gate_turn, apart=b != 1)

            for piece in range(4, OUT_PIECES):
                split_out_lo(dve, piece)
            for j in range(KC):
                split_m_lo(dve, j, 1)

            dve.wait_ge(rows1_loaded, 32)
            for t in range(T_TILES):
                dve.wait_ge(skip_loaded[t % SKIP_SLOTS], 16 * (t // SKIP_SLOTS + 1))
                width = HALF if t < T_TILES - 1 else HALF // 2
                if t >= 2:
                    dve.wait_ge(stored[t % 2], 16 * (t // 2))
                for n, (a, b) in enumerate(out_parts(t)):
                    dve.wait_ge(out_done, out_count(t, a // HALF) + (n == 2))
                    v.tensor_tensor(res[:, t % 2, a:b], PS[:, part_bank(t, n), 0:b - a],
                                    skip[:, t % SKIP_SLOTS, a:b], ALU.add).then_inc(res_half, 1)
                    dve.wait_ge(res_half, 2 * t + n + 1)
                    for c in range(a, b, width):
                        then(v.bn_stats(stats2[:, t, c // width, :], res[:, t % 2, c:c + width]))
                v.bn_aggr(mv2[:, t, :], stats2[:, t, 0:D // width, :]).then_inc(mean_ready, 1)
                dve.wait_ge(mean_ready, t + 1)
                var, root, r, a = (small2[:, n, t:t + 1] for n in range(4))
                v.tensor_scalar(var, mv2[:, t, 1:2], LN_EPS, None, ALU.add).then_inc(var2_ready, 1)
                then(v.scalar_tensor_tensor(res[:, t % 2, :], res[:, t % 2, :], mv2[:, t, 0:1], gain1,
                                            ALU.subtract, ALU.mult))
                dve.wait_ge(var2_ready, t + 1)
                dve.wait_ge(root2_ready, t + 1)
                rsqrt(var, root, r, a)
                for part in ((0, D),) if t < T_TILES - 1 else ((0, HALF), (HALF, D)):
                    rows = res[:, t % 2, slice(*part)]
                    v.scalar_tensor_tensor(rows, rows, r, bias1[:, slice(*part)], ALU.mult, ALU.add)\
                        .then_inc(row_ready, 1)

        @block.tensor
        def _(pe):
            mm = nc.tensor.matmul
            turn = nc.tensor.transpose

            pe.wait_ge(ident_ready, 2)
            pe.wait_ge(params_loaded, 16 * 5)
            turn(PS[:, 7, 0:N_ROWS], prow, ident[0:N_ROWS, 0:N_ROWS]).then_inc(params_turned, 1)
            def turn_z(blocks):
                for n in blocks:
                    half, k = n // KC, n % KC
                    pe.wait_ge(z_by_act, 2)
                    pe.wait_ge(z_by_dve, (2, 6)[half])
                    if n >= 4:
                        wait_hf(pe, n - 4)
                    for t in range(4):
                        last = turn(PS[:, 3 + n % 4, P * t:P * t + P], xin[:, 4 * half + t, P * k:P * k + P],
                                    ident[:])
                    last.then_inc(z_turned, 1)

            def turn_z_meta():
                pe.wait_ge(z_by_act, 3)
                pe.wait_ge(params_ready, 1)
                for k in range(KC):
                    last = turn(PS[:, 7, P + META * k:P + META * k + META], xmeta[:, P * k:P * k + P],
                                ident[0:META, 0:META])
                last.then_inc(z_turned, 1)

            def three_passes(dst, w_parts, x_parts, n_k, begin=True, end=True, before=None):
                (wh, wl), (xh, xl) = w_parts, x_parts
                for k in range(n_k):
                    if before:
                        before(k)
                    for p, (a, b) in enumerate(((wh, xh), (wh, xl), (wl, xh))):
                        last = mm(dst, a(k), b(k), start=begin and k == 0 and p == 0,
                                  stop=end and k == n_k - 1 and p == 2)
                return last

            def project(sec, i, g, slot, tokens, more=0, before=None):
                b = sec.banks[g]
                a, z = tokens
                wait(pe, bank_read[b], sec.used(i, g) + more)
                three_passes(PS[:, b, 0:z - a],
                             (lambda k: w_hi[:, slot, k, :], lambda k: w_lo[:, slot, k, :]),
                             (lambda k: h_hi[:, k, a:z], lambda k: h_lo[:, k, a:z]), KC, before=before)\
                    .then_inc(groups_done, 1)

            turn_z(range(KC))

            def first_half(k):
                if k == KC - 1:
                    turn_z(range(KC, KC + 4))
                wait_lo(pe, k)

            def turn_rest(k):
                if k == 2:
                    turn_z(range(KC + 4, 2 * KC))

            def second_half(k):
                wait_lo(pe, KC + k)

            for i in range(2):
                for g in range(4):
                    n, c = g % 2, g // 2
                    if c == 0:
                        pe.wait_ge(w_lo_ready, Q.tile(i, n) + 1)
                    before = (first_half, turn_rest, second_half, None)[g] if i == 0 else None
                    project(Q, i, g, n, REAL_ONLY[c], before=before)
                    if i == 0 and g == 2:
                        turn_z_meta()
            pe.wait_ge(meta_lo_ready, 1)
            for n in range(2):
                pe.wait_ge(w_lo_ready, KV.tile(0, n) + 1)
                for c in range(3):
                    project(KV, 0, 3 * n + c, n, WITH_META[c])

            def turn_v_windows():
                for b in range(3):
                    pe.wait_ge(bank_read[b], KV.used_end[b])
                for c in range(N_CHUNKS):
                    last = turn(PS[:, V_BANKS[c // 4], P * (c % 4):P * (c % 4) + P],
                                vT[:, META + CHUNK * c:META + CHUNK * c + P], ident[:])
                    if c % 4 == 3:
                        last.then_inc(v_turned, 1)

            def turn_v_meta(k):
                if k != 1:
                    return
                pe.wait_ge(v_win_ready, 4)
                turn(PS[0:2 * META, 7, 0:P], vT_meta_bd[:], ident[:]).then_inc(v_turned, 1)

            pe.wait_ge(zeroed, N_ZEROED)
            pe.wait_ge(meta_staged, 4)

            def scores(i, n):
                chunk = i * 4 + n
                pe.wait_ge(qk_staged, chunk * 3 + 3)
                pe.wait_ge(q_lo_staged, chunk + 1)
                wait(pe, probs_ready, chunk * 4)
                for c in range(2):
                    for p, (a, b) in enumerate(PASSES):
                        last = mm(S_PS[:, c, :], q_stage[:, a, 2 * c:2 * c + 2, :].rearrange("p t q -> p (t q)"),
                                  k_stage[:, b, :], start=p == 0, stop=p == 2)
                last.then_inc(scores_done, 1)

            def turn_probs(i, n):
                chunk = i * 4 + n
                pe.wait_ge(probs_scaled, chunk + 1)
                wait(pe, pT_ready, chunk)
                wait(pe, pT_meta_ready, chunk)
                for c in range(2):
                    for g in range(2):
                        turn(PT_PS[:, g, P * c:P * c + P], probs[:, c, WIN_COLS[g]], ident[:])
                    last = turn(PTM_PS[:, P * c:P * c + P], probs[:, c, META_COLS], ident[:])
                last.then_inc(probs_turned, 1)

            def times_v(i, n):
                chunk = i * 4 + n
                pe.wait_ge(v_staged, chunk * 2 + 2)
                pe.wait_ge(pT_ready, chunk + 1)
                pe.wait_ge(pT_meta_ready, chunk + 1)
                pe.wait_ge(pT_meta_hi_copied, chunk + 1)
                wait(pe, o_ready, chunk)
                out_at = PS[:, 7, 0:4 * CHUNK]
                mm(out_at, v_meta[:], pT_meta[:], start=True, stop=False)
                for g in range(2):
                    for p, (a, b) in enumerate(PASSES):
                        last = mm(out_at, v_stage[:, a, g:g + 2, :].rearrange("p z d -> p (z d)"),
                                  pT[:, b, g, :], start=False, stop=g == 1 and p == 2)
                last.then_inc(o_done, 1)

            def mix_turn(i, first=False):
                for g in range(11):
                    tile, c = min(g // 3, 3), g - 3 * min(g // 3, 3)
                    if c == 0:
                        pe.wait_ge(w_lo_ready, MIX.tile(i, tile) + 1)
                    if first and g == 2:
                        pe.wait_ge(v_win_ready, V_BANKS.index(MIX.banks[2]) + 1)
                    project(MIX, i, g, tile % 2, (WITH_META, FOR_CONV, FOR_CONV, REAL_ONLY)[tile][c],
                            before=turn_v_meta if first and g == 2 else None)
                    if first and g == 0:
                        turn_v_windows()
                    if g in TIMES_V_AFTER:
                        if first and g == TIMES_V_AFTER[0]:
                            pe.wait_ge(v_meta_ready, 1)
                        times_v(i, TIMES_V_AFTER.index(g))
                    if g in TURN_AFTER:
                        turn_probs(i, TURN_AFTER.index(g))
                    if g in SCORES_AFTER:
                        scores(i, SCORES_AFTER.index(g))

            mix_turn(0, first=True)
            with pe.Fori(1, 4) as i:
                mix_turn(i)

            pe.wait_ge(pool_w_loaded, 16)
            pe.wait_ge(pooled_ready, 4)
            pe.wait_ge(probs_ready, 4 * N_CHUNKS)
            for n in range(8):
                g, c = n // 2, n % 2
                pe.wait_ge(bank_read[MAP.banks[n]], MAP.used(0, n))
                mm(PS[:, MAP.banks[n], :], pool_wt[:, g, :], pooled[:, g, HALF * c:HALF * c + HALF],
                   start=True, stop=True).then_inc(groups_done, 1)

            with pe.Fori(0, N_BRANCH) as b:
                with pe.Fori(0, 2) as i:
                    for n in range(2):
                        pe.wait_ge(w_lo_ready, b * BRANCH_TILES + Z[0].tile(i, n) + 1)
                        for c in range(2):
                            project(Z[0], i, 2 * n + c, n, REAL_ONLY[c], more=b * BRANCH_USES)
                with pe.Fori(0, 2) as i:
                    for pair in range(2):
                        for n in range(2):
                            tile = 3 * pair + n
                            pe.wait_ge(w_lo_ready, b * BRANCH_TILES + GATE[0].tile(i, tile) + 1)
                            for c in range(2):
                                project(GATE[0], i, 8 * pair + 2 * n + c, tile % 2, REAL_ONLY[c],
                                        more=b * BRANCH_USES)
                        tile = 3 * pair + 2
                        pe.wait_ge(w_lo_ready, b * BRANCH_TILES + GATE[0].tile(i, tile) + 1)
                        pe.wait_ge(y_lo_ready, b * 8 + 8)
                        wh, wl = (w[:, tile % 2, :, :].rearrange("p (k two) c -> p k (two c)", two=2)
                                  for w in (w_hi, w_lo))
                        for n in range(2):
                            for c in range(2):
                                g = 8 * pair + 4 + 2 * n + c
                                bank = GATE[0].banks[g]
                                pe.wait_ge(bank_read[bank], GATE[0].used(i, g) + b * BRANCH_USES)
                                three_passes(PS[:, bank, :],
                                             (lambda k: wh[:, k, P * n:P * n + P],
                                              lambda k: wl[:, k, P * n:P * n + P]),
                                             (lambda k: y_hi[:, k, HALF * c:HALF * c + HALF],
                                              lambda k: y_lo[:, k, HALF * c:HALF * c + HALF]), 4)\
                                    .then_inc(groups_done, 1)

            def out_rows_product(t, h, k0, k1, part=(0, HALF)):
                a, b = part
                bank = out_bank(t, h) + (a > 0)
                tokens = slice(META + P * t, META + P * t + P)
                return three_passes(PS[:, bank, 0:b - a],
                                    (lambda k: h_hi[:, k0 + k, tokens], lambda k: h_lo[:, k0 + k, tokens]),
                                    (lambda k: wo_hi[h][:, k0 + k, a:b], lambda k: wo_lo[h][:, k0 + k, a:b]),
                                    k1 - k0, begin=k0 == 0, end=k1 == KC)

            for n in range(OUT_PIECES):
                h, k = n // 4, 2 * (n % 4)
                pe.wait_ge(wo_lo_ready, n + 1)
                if h == 0:
                    pe.wait_ge(m_lo_ready, k + 2)
                for t in range(SIDE):
                    last = out_rows_product(t, h, k, k + 2)
                    if k == KC - 2:
                        last.then_inc(out_done, 1)
            for t in range(SIDE, T_TILES):
                if t == 4:
                    pe.wait_ge(m_lo_ready, 2 * KC)
                for n, (a, b) in enumerate(out_parts(t)):
                    h = a // HALF
                    bank = part_bank(t, n)
                    if t < 4:
                        pe.wait_ge(bank_read[bank], GATE[-1].used_end[bank])
                    else:
                        pe.wait_ge(res_half, 2 * (t - 4) + n + 1)
                    out_rows_product(t, h, 0, KC, (a % HALF, a % HALF + b - a)).then_inc(out_done, 1)


_INS = ['x', 'meta_tokens', 'ln0_g', 'ln0_b', 'w_in', 'b_gate', 'conv_w', 'attn_sinks', 'pool_w', 'pool_scale',
        'w_br_a', 'w_br_b', 'w_br_c', 'w_out', 'ln_g', 'ln_b']
_OUTS = [((1, 1024, 1024), 'float32')]


def kernel(**inputs):
    import numpy as _np
    import concourse.bacc as _bacc
    from concourse import mybir as _mybir
    from concourse.bass_utils import run_bass_kernel_spmd as _run

    nc = _bacc.Bacc("TRN2", target_bir_lowering=False, num_devices=1)
    arrays, args = {}, []
    for name in _INS:
        a = _np.ascontiguousarray(inputs[name])
        arrays[f"in_{name}_dram"] = a
        args.append(nc.dram_tensor(f"in_{name}_dram", a.shape, _mybir.dt.from_np(a.dtype), kind="ExternalInput").ap())
    for i, (shape, dtype) in enumerate(_OUTS):
        dt = _mybir.dt.from_np(_np.dtype(dtype))
        args.append(nc.dram_tensor(f"out_{i}_dram", shape, dt, kind="ExternalOutput").ap())
    hybrid_layer(nc, *args)
    r = _run(nc, [arrays], core_ids=[0])
    return r.results[0]["out_0_dram"]
```
